# Optimizing a Trainium2 kernel written in Bass

```python
import math
import jax, jax.numpy as jnp
from jax import lax
import numpy as np

D_MODEL = 1024
BATCH = 1
SEQ = 128
DEPTH = 2
DEC_BATCH = 1
DEC_SEQ = 512
PAST_LEN = 128

GRID_W = 64
N_MIXERS = 2
N_ATTN_LAYERS = (DEPTH + N_MIXERS - 1) // N_MIXERS
N_SSD_LAYERS = DEPTH // N_MIXERS
N_HEADS = 16
N_KV_HEADS = 4
HEAD_DIM = D_MODEL // N_HEADS
KV_REP = N_HEADS // N_KV_HEADS
ROPE_THETA = 10000.0
Q_BLOCK = 128
SSD_EXPAND = 2
D_INNER = SSD_EXPAND * D_MODEL
SSD_HEAD_DIM = 64
SSD_HEADS = D_INNER // SSD_HEAD_DIM
SSD_GROUPS = 4
SSD_REP = SSD_HEADS // SSD_GROUPS
D_STATE = 128
D_CONV = 5
CHUNK = 128
CONV_DIM = D_INNER + 2 * SSD_GROUPS * D_STATE
IN_PROJ_DIM = D_INNER + CONV_DIM + 2 * SSD_HEADS
N_EXPERTS = 16
N_EXPERT_GROUPS = 4
EXPERTS_PER_GROUP = N_EXPERTS // N_EXPERT_GROUPS
TOP_K = 2
D_FF_EXPERT = D_MODEL // 4
EPS = 1e-6

kernel_name = "hybrid_gqa_ssd_moe_diffusion_step"

F32 = jnp.float32

def rms_norm(x, g):
    xf = x.astype(F32)
    y = xf * lax.rsqrt(jnp.mean(xf * xf, axis=-1, keepdims=True) + EPS)
    return (y * g.astype(F32)).astype(x.dtype)

def modulation(cond, w, b):
    m = jax.nn.silu(cond) @ w + b
    return jnp.split(m, 6, axis=-1)

def adaln(x, g, shift, scale):
    return rms_norm(x, g) * (1 + scale) + shift

def axial_rope_tables(t_len):
    rows = t_len // GRID_W
    row_ids = jnp.repeat(jnp.arange(rows), GRID_W).astype(F32)
    col_ids = jnp.tile(jnp.arange(GRID_W), rows).astype(F32)
    n_freq = HEAD_DIM // 4
    inv = 1.0 / (ROPE_THETA ** (jnp.arange(n_freq, dtype=F32) / n_freq))
    ang = jnp.concatenate([row_ids[:, None] * inv, col_ids[:, None] * inv], axis=-1)
    return jnp.cos(ang), jnp.sin(ang)

def apply_rope(x, cos, sin):
    xf = x.astype(F32)
    x1, x2 = jnp.split(xf, 2, axis=-1)
    cs, sn = cos[None, :, None, :], sin[None, :, None, :]
    return jnp.concatenate([x1 * cs - x2 * sn, x2 * cs + x1 * sn], axis=-1).astype(x.dtype)

def blocked_attention(q, k, v):
    b, tq = q.shape[0], q.shape[1]
    nb = tq // Q_BLOCK
    qb = q.reshape(b, nb, Q_BLOCK, N_KV_HEADS, KV_REP, HEAD_DIM).transpose(1, 0, 2, 3, 4, 5)
    scale = HEAD_DIM ** -0.5

    def one_block(qblk):
        s = jnp.einsum('bqgrd,bkgd->bgrqk', qblk, k, preferred_element_type=F32) * scale
        p = jax.nn.softmax(s, axis=-1).astype(v.dtype)
        return jnp.einsum('bgrqk,bkgd->bqgrd', p, v)

    o = lax.map(one_block, qb)
    return o.transpose(1, 0, 2, 3, 4, 5).reshape(b, tq, N_HEADS * HEAD_DIM)

def qkv_project(h, w_qkv, q_g, k_g):
    b, t, _ = h.shape
    qkv = h @ w_qkv
    q, k, v = jnp.split(qkv, [N_HEADS * HEAD_DIM, (N_HEADS + N_KV_HEADS) * HEAD_DIM], axis=-1)
    q = rms_norm(q.reshape(b, t, N_HEADS, HEAD_DIM), q_g)
    k = rms_norm(k.reshape(b, t, N_KV_HEADS, HEAD_DIM), k_g)
    v = v.reshape(b, t, N_KV_HEADS, HEAD_DIM)
    return q, k, v

def attn_context(h, w_qkv, q_g, k_g, w_o):
    b, t, _ = h.shape
    q, k, v = qkv_project(h, w_qkv, q_g, k_g)
    o = blocked_attention(q.reshape(b, t, N_KV_HEADS, KV_REP, HEAD_DIM), k, v)
    return o @ w_o, k, v

def attn_latent(h, ctx_k, ctx_v, w_qkv, q_g, k_g, w_o):
    b, t, _ = h.shape
    q, k, v = qkv_project(h, w_qkv, q_g, k_g)
    cos, sin = axial_rope_tables(t)
    q = apply_rope(q, cos, sin)
    k = apply_rope(k, cos, sin)
    k_all = jnp.concatenate([k, ctx_k.astype(k.dtype)], axis=1)
    v_all = jnp.concatenate([v, ctx_v.astype(v.dtype)], axis=1)
    o = blocked_attention(q.reshape(b, t, N_KV_HEADS, KV_REP, HEAD_DIM), k_all, v_all)
    return o @ w_o

def dwconv_centred(u, w, bias):
    out = lax.conv_general_dilated(
        u, w[:, None, :].astype(u.dtype), window_strides=(1,),
        padding=[(D_CONV // 2, D_CONV // 2)],
        dimension_numbers=('NWC', 'WIO', 'NWC'),
        feature_group_count=u.shape[-1])
    return out + bias

def ssd_scan(x, dt, a, bm, cm, init):
    b, L = x.shape[0], x.shape[1]
    nc = L // CHUNK
    xs = (x * dt[..., None]).reshape(b, nc, CHUNK, SSD_GROUPS, SSD_REP, SSD_HEAD_DIM)
    da = (dt * a).reshape(b, nc, CHUNK, SSD_GROUPS, SSD_REP)
    bc = bm.reshape(b, nc, CHUNK, SSD_GROUPS, D_STATE)
    cc = cm.reshape(b, nc, CHUNK, SSD_GROUPS, D_STATE)
    acum = jnp.cumsum(da, axis=2)
    seg = acum[:, :, :, None] - acum[:, :, None, :]
    causal = jnp.tril(jnp.ones((CHUNK, CHUNK), dtype=bool))
    lmat = jnp.exp(jnp.where(causal[:, :, None, None], seg, -jnp.inf))
    cb = jnp.einsum('bcqgn,bcsgn->bcqsg', cc, bc)
    y_diag = jnp.einsum('bcqsgr,bcsgrp->bcqgrp', cb[..., None] * lmat, xs)
    decay = jnp.exp(acum[:, :, -1:] - acum)
    states = jnp.einsum('bcsgn,bcsgrp->bcgrpn', bc, xs * decay[..., None])
    chunk_decay = jnp.exp(acum[:, :, -1])

    def step(hstate, inp):
        st, dec = inp
        return hstate * dec[..., None, None] + st, hstate

    h0 = init.astype(F32).reshape(b, SSD_GROUPS, SSD_REP, SSD_HEAD_DIM, D_STATE)
    final, prev = lax.scan(step, h0, (jnp.moveaxis(states, 1, 0), jnp.moveaxis(chunk_decay, 1, 0)))
    prev = jnp.moveaxis(prev, 0, 1)
    y_off = jnp.einsum('bcqgn,bcgrpn->bcqgrp', cc, prev) * jnp.exp(acum)[..., None]
    y = (y_diag + y_off).reshape(b, L, SSD_HEADS, SSD_HEAD_DIM)
    return y, final.reshape(b, SSD_HEADS, SSD_HEAD_DIM, D_STATE)

def ssd_mixer(h, init_f, init_b, in_proj, conv_w, conv_b, dt_bias, a_log, d_skip, norm_g, out_proj):
    b, L, _ = h.shape
    zxbcdt = h @ in_proj
    z, xbc, dt = jnp.split(zxbcdt, [D_INNER, D_INNER + CONV_DIM], axis=-1)
    xbc = jax.nn.silu(dwconv_centred(xbc, conv_w, conv_b))
    x, bm, cm = jnp.split(xbc, [D_INNER, D_INNER + SSD_GROUPS * D_STATE], axis=-1)
    x = x.reshape(b, L, SSD_HEADS, SSD_HEAD_DIM).astype(F32)
    bm = bm.reshape(b, L, SSD_GROUPS, D_STATE).astype(F32)
    cm = cm.reshape(b, L, SSD_GROUPS, D_STATE).astype(F32)
    dt = jax.nn.softplus(dt.astype(F32).reshape(b, L, 2, SSD_HEADS) + dt_bias.astype(F32))
    a = -jnp.exp(a_log.astype(F32))
    flip = lambda t: jnp.flip(t, axis=1)
    y_f, s_f = ssd_scan(x, dt[:, :, 0], a[0], bm, cm, init_f)
    y_b, s_b = ssd_scan(flip(x), flip(dt[:, :, 1]), a[1], flip(bm), flip(cm), init_b)
    y = y_f + flip(y_b) + x * d_skip.astype(F32)[:, None]
    y = y.reshape(b, L, D_INNER).astype(h.dtype)
    y = rms_norm(y * jax.nn.silu(z), norm_g)
    return y @ out_proj, jnp.stack([s_f, s_b], axis=1)

def moe(h, router_w, router_b, w_gate, w_up, w_down):
    shp = h.shape
    t = h.reshape(-1, D_MODEL)
    scores = jax.nn.sigmoid((t @ router_w).astype(F32))
    biased = scores + router_b.astype(F32)
    grp = biased.reshape(-1, N_EXPERT_GROUPS, EXPERTS_PER_GROUP)
    grp_score = jnp.sum(lax.top_k(grp, TOP_K)[0], axis=-1)
    sel = jnp.argmax(grp_score, axis=-1)
    in_grp = (jnp.arange(N_EXPERTS) // EXPERTS_PER_GROUP)[None, :] == sel[:, None]
    _, idx = lax.top_k(jnp.where(in_grp, biased, -jnp.inf), TOP_K)
    w = jnp.take_along_axis(scores, idx, axis=-1)
    w = w / jnp.sum(w, axis=-1, keepdims=True)
    gates = jnp.sum(jax.nn.one_hot(idx, N_EXPERTS, dtype=F32) * w[..., None], axis=1)
    hg = jnp.einsum('td,edf->tef', t, w_gate)
    hu = jnp.einsum('td,edf->tef', t, w_up)
    act = jax.nn.silu(hg) * hu * gates[..., None].astype(t.dtype)
    out = jnp.einsum('tef,efd->td', act, w_down)
    return out.reshape(shp)

def setup_inputs(seed: int = 0) -> dict:
    key = jax.random.key(seed)
    ks = jax.random.split(key, 32)
    nrm = lambda k, shape, s: jax.random.normal(k, shape, F32) * s
    dt_min, dt_max = 0.001, 0.1
    u = jax.random.uniform(ks[20], (N_SSD_LAYERS, 2, SSD_HEADS), F32)
    dt0 = jnp.exp(u * (math.log(dt_max) - math.log(dt_min)) + math.log(dt_min))
    dt_bias = dt0 + jnp.log(-jnp.expm1(-dt0))
    a_log = jnp.log(jax.random.uniform(ks[21], (N_SSD_LAYERS, 2, SSD_HEADS), F32, 1.0, 16.0))
    return {
        "x_prompt": nrm(ks[0], (BATCH, SEQ, D_MODEL), 1.0),
        "x_sample": nrm(ks[1], (DEC_BATCH, DEC_SEQ, D_MODEL), 1.0),
        "c": nrm(ks[2], (DEC_BATCH, D_MODEL), 1.0),
        "c_ctx": nrm(ks[3], (D_MODEL,), 1.0),
        "cache_k": nrm(ks[4], (DEC_BATCH, N_ATTN_LAYERS, PAST_LEN, N_KV_HEADS, HEAD_DIM), 1.0),
        "cache_v": nrm(ks[5], (DEC_BATCH, N_ATTN_LAYERS, PAST_LEN, N_KV_HEADS, HEAD_DIM), 1.0),
        "state_ssm": nrm(ks[6], (DEC_BATCH, N_SSD_LAYERS, 2, SSD_HEADS, SSD_HEAD_DIM, D_STATE), 0.1),
        "mod_w": nrm(ks[7], (DEPTH, D_MODEL, 6 * D_MODEL), 0.5 * D_MODEL ** -0.5),
        "mod_b": nrm(ks[8], (DEPTH, 6 * D_MODEL), 0.01),
        "norm1_g": 1.0 + nrm(ks[9], (DEPTH, D_MODEL), 0.01),
        "norm2_g": 1.0 + nrm(ks[10], (DEPTH, D_MODEL), 0.01),
        "attn_w_qkv": nrm(ks[11], (N_ATTN_LAYERS, D_MODEL, (N_HEADS + 2 * N_KV_HEADS) * HEAD_DIM), D_MODEL ** -0.5),
        "attn_q_norm_g": 1.0 + nrm(ks[12], (N_ATTN_LAYERS, HEAD_DIM), 0.01),
        "attn_k_norm_g": 1.0 + nrm(ks[13], (N_ATTN_LAYERS, HEAD_DIM), 0.01),
        "attn_w_o": nrm(ks[14], (N_ATTN_LAYERS, N_HEADS * HEAD_DIM, D_MODEL), (N_HEADS * HEAD_DIM) ** -0.5),
        "ssd_in_proj": nrm(ks[15], (N_SSD_LAYERS, D_MODEL, IN_PROJ_DIM), D_MODEL ** -0.5),
        "ssd_conv_w": nrm(ks[16], (N_SSD_LAYERS, D_CONV, CONV_DIM), D_CONV ** -0.5),
        "ssd_conv_b": nrm(ks[17], (N_SSD_LAYERS, CONV_DIM), 0.01),
        "ssd_dt_bias": dt_bias,
        "ssd_a_log": a_log,
        "ssd_d": 1.0 + nrm(ks[18], (N_SSD_LAYERS, SSD_HEADS), 0.01),
        "ssd_norm_g": 1.0 + nrm(ks[19], (N_SSD_LAYERS, D_INNER), 0.01),
        "ssd_out_proj": nrm(ks[22], (N_SSD_LAYERS, D_INNER, D_MODEL), D_INNER ** -0.5),
        "router_w": nrm(ks[23], (D_MODEL, N_EXPERTS), D_MODEL ** -0.5),
        "router_b": nrm(ks[24], (N_EXPERTS,), 0.01),
        "expert_w_gate": nrm(ks[25], (DEPTH, N_EXPERTS, D_MODEL, D_FF_EXPERT), D_MODEL ** -0.5),
        "expert_w_up": nrm(ks[26], (DEPTH, N_EXPERTS, D_MODEL, D_FF_EXPERT), D_MODEL ** -0.5),
        "expert_w_down": nrm(ks[27], (DEPTH, N_EXPERTS, D_FF_EXPERT, D_MODEL), D_FF_EXPERT ** -0.5),
    }

def reference(x_prompt, x_sample, c, c_ctx, cache_k, cache_v, state_ssm,
              mod_w, mod_b, norm1_g, norm2_g,
              attn_w_qkv, attn_q_norm_g, attn_k_norm_g, attn_w_o,
              ssd_in_proj, ssd_conv_w, ssd_conv_b, ssd_dt_bias, ssd_a_log, ssd_d, ssd_norm_g, ssd_out_proj,
              router_w, router_b, expert_w_gate, expert_w_up, expert_w_down):
    xp, xs = x_prompt, x_sample
    cond_p = c_ctx[None, None, :]
    cond_s = c[:, None, :]
    zero_state = jnp.zeros((xp.shape[0], SSD_HEADS, SSD_HEAD_DIM, D_STATE), F32)
    new_k, new_v, new_ssm = [], [], []
    for layer in range(DEPTH):
        sh1p, sc1p, g1p, sh2p, sc2p, g2p = modulation(cond_p, mod_w[layer], mod_b[layer])
        sh1s, sc1s, g1s, sh2s, sc2s, g2s = modulation(cond_s, mod_w[layer], mod_b[layer])
        hp = adaln(xp, norm1_g[layer], sh1p, sc1p)
        hs = adaln(xs, norm1_g[layer], sh1s, sc1s)
        i = layer // N_MIXERS
        if layer % N_MIXERS == 0:
            yp, kp, vp = attn_context(hp, attn_w_qkv[i], attn_q_norm_g[i], attn_k_norm_g[i], attn_w_o[i])
            ys = attn_latent(hs, cache_k[:, i], cache_v[:, i], attn_w_qkv[i], attn_q_norm_g[i],
                             attn_k_norm_g[i], attn_w_o[i])
            new_k.append(kp)
            new_v.append(vp)
        else:
            yp, sp = ssd_mixer(hp, zero_state, zero_state, ssd_in_proj[i], ssd_conv_w[i], ssd_conv_b[i],
                               ssd_dt_bias[i], ssd_a_log[i], ssd_d[i], ssd_norm_g[i], ssd_out_proj[i])
            ys, _ = ssd_mixer(hs, state_ssm[:, i, 0], state_ssm[:, i, 1], ssd_in_proj[i], ssd_conv_w[i],
                              ssd_conv_b[i], ssd_dt_bias[i], ssd_a_log[i], ssd_d[i], ssd_norm_g[i],
                              ssd_out_proj[i])
            new_ssm.append(sp)
        xp = xp + g1p * yp
        xs = xs + g1s * ys
        xp = xp + g2p * moe(adaln(xp, norm2_g[layer], sh2p, sc2p), router_w, router_b,
                            expert_w_gate[layer], expert_w_up[layer], expert_w_down[layer])
        xs = xs + g2s * moe(adaln(xs, norm2_g[layer], sh2s, sc2s), router_w, router_b,
                            expert_w_gate[layer], expert_w_up[layer], expert_w_down[layer])
    new_cache_k = jnp.stack(new_k, axis=1)
    new_cache_v = jnp.stack(new_v, axis=1)
    new_state_ssm = jnp.stack(new_ssm, axis=1)
    return (xp, xs, new_cache_k, new_cache_v, new_state_ssm)


_drawn_inputs = setup_inputs


def setup_inputs(seed=0):
    import zlib

    import numpy as np

    out = dict(_drawn_inputs(seed))
    spreads = {}
    factors = {'norm1_g': 3.299,
     'attn_q_norm_g': 8.0,
     'attn_k_norm_g': 5.604,
     'ssd_conv_b': 12.507,
     'ssd_d': 42.56,
     'ssd_norm_g': 26.091,
     'state_ssm': 8.0}
    for name, (base, spread) in spreads.items():
        noise = np.random.default_rng([zlib.crc32(name.encode()), seed]).standard_normal(out[name].shape)
        drawn = base * np.exp(spread * noise) if base else spread * noise
        out[name] = __import__('jax').numpy.asarray(drawn.astype(out[name].dtype))
    for name, factor in factors.items():
        out[name] = (out[name] * factor).astype(out[name].dtype)
    return out
```

```python
import math
import numpy as np
import concourse.bass as bass
from concourse import mybir
from contextlib import ExitStack

F32 = mybir.dt.float32
I32 = mybir.dt.int32
U32 = mybir.dt.uint32
ALU = mybir.AluOpType
ACT = mybir.ActivationFunctionType
AX = mybir.AxisListType

P = 128
D = 1024
KD = D // P
SEQ, DEC = 128, 512
TOK = SEQ + DEC
NT = TOK // P
PAST = 128
GRID_W = 64
NH, NKV, HD = 16, 4, 64
QK = (NH + NKV) * HD
DI = 2048
SH, SG, SP, SN = 32, 4, 64, 128
HG = SH // SG
NE, NG, EG = 16, 4, 4
FF = D // 4
EPS = 1e-6
MAXT = (2 * TOK - NE) // P + NE + 1
MAXT += MAXT % 2
PG = 1024

T_ID, T_UP, T_LOW, T_GT, T_LT, T_ONE = (i * P for i in range(6))
T_COS = 6 * P
T_SIN = T_COS + (NT - 1) * HD
T_IOTA = T_SIN + (NT - 1) * HD
T_TIE = T_IOTA + MAXT
T_END = T_TIE + NE


def tables():
    t = np.zeros((P, T_END), np.float32)
    r, c = np.arange(P)[:, None], np.arange(P)[None, :]
    for at, m in ((T_ID, r == c), (T_UP, r <= c), (T_LOW, r >= c), (T_GT, r > c), (T_LT, r < c), (T_ONE, r >= 0)):
        t[:, at:at + P] = m
    n_freq = HD // 4
    inv = (1.0 / (np.float32(10000.0) ** (np.arange(n_freq, dtype=np.float32) / n_freq))).astype(np.float32)
    pos = np.arange(DEC)
    ang = np.concatenate([(pos // GRID_W)[:, None].astype(np.float32) * inv,
                          (pos % GRID_W)[:, None].astype(np.float32) * inv], axis=1)
    cs = np.cos(ang).reshape(NT - 1, P, 2 * n_freq).transpose(1, 0, 2)
    sn = np.sin(ang).reshape(NT - 1, P, 2 * n_freq).transpose(1, 0, 2)
    t[:, T_COS:T_SIN] = np.concatenate([cs, cs], axis=2).reshape(P, -1)
    t[:, T_SIN:T_IOTA] = np.concatenate([-sn, sn], axis=2).reshape(P, -1)
    t[:, T_IOTA:T_TIE] = np.arange(MAXT)[None, :]
    e = np.arange(EG)
    t[:, T_TIE:T_END] = (e[None, :] < e[:, None]).reshape(1, -1)
    return t


class Order:

    def __init__(self, eng, sem):
        self.eng, self.sem, self.n = eng, sem, 0

    def __call__(self, ins):
        ins.then_inc(self.sem, 1)
        self.n = self.n + 1
        self.eng.wait_ge(self.sem, self.n)


def backbone(nc, x_prompt, x_sample, c, c_ctx, cache_k, cache_v, state_ssm, mod_w, mod_b, norm1_g, norm2_g,
             w_qkv, q_g, k_g, w_o, in_proj, conv_w, conv_b, dt_bias, a_log, ssd_d, ssd_g, out_proj,
             router_w, router_b, w_gate, w_up, w_down, consts,
             y_prompt, y_sample, new_k, new_v, new_ssm):
    mod_d = nc.dram_tensor("mod_rows", (2, 2, 3, 2, D), F32, kind="Internal").ap()
    ctx = ExitStack()
    with ctx:
        def sb(name, shape, dt=F32):
            return ctx.enter_context(nc.sbuf_tensor(name, shape, dt))

        def sem(name):
            return ctx.enter_context(nc.semaphore(name))

        def sems(name, n):
            return [sem(f"{name}{i}") for i in range(n)]

        mem = sb("mem", [P, 50 * PG])
        tab = sb("tab", [P, T_END])
        ps = ctx.enter_context(nc.psum_tensor("ps", [P, 8, 512], F32))
        psf = ps[:, :, :].rearrange("p b n -> p (b n)")

        def page(at, n, parts=P):
            a = int(at * PG)
            return mem[0:parts, a:a + n]

        ident = tab[:, T_ID:T_ID + P]
        X = page(0, NT * D).rearrange("p (t n) -> p t n", t=NT)
        HT = page(5, KD * TOK).rearrange("p (k n) -> p k n", k=KD)
        WS = [page(10 + 4 * i, 4 * PG).rearrange("p (k n) -> p k n", k=KD) for i in range(3)]
        MB = [page(22 + 6 * i, 6 * D).rearrange("p (f c n) -> p f c n", f=3, c=2) for i in range(2)]
        condr = sb("condr", [16, P])
        condT = sb("condT", [P, 2, KD])
        MR = page(34, 12 * D, 2).rearrange("p (l n) -> p l n", l=2)
        H = page(34, NT * D).rearrange("p (t n) -> p t n", t=NT)
        SQX = H[:, NT - 1, :]
        JUNK, G = page(39, D), page(40, D)
        ssq = sb("ssq", [P, 8])
        V = page(34, 6 * 256).rearrange("p (t n) -> p t n", t=6)
        QN = page(35.5, QK)
        SQ = page(36.75, QK)
        T2 = page(38, QK)
        QF = page(39.25, D)
        KDUP = page(40.25, 512).rearrange("p (g two d) -> p g two d", g=NKV, two=2)
        KDC = page(49, 512).rearrange("p (g two d) -> p g two d", g=NKV, two=2)
        KOUT = page(49.5, 256)
        QT = page(41, 8 * TOK).rearrange("p (m n) -> p m n", m=8)
        KT = page(46, 4 * 768).rearrange("p (g n) -> p g n", g=4)
        gqk = sb("gqk", [P, 2, HD])
        rs = sb("rs", [P, NH + NKV])
        PR = [page(35.5 + 0.625 * i, 640) for i in range(2)]
        PT = [page(36.75 + 0.625 * i, 640) for i in range(2)]
        QC = page(39.25, D).rearrange("p (m n) -> p m n", m=8)
        OA = page(28, NT * D).rearrange("p (t n) -> p t n", t=NT)
        nmx = sb("nmx", [P, NH])
        den = sb("den", [P, NH])
        rden = sb("rden", [P, NH])

        RW = sb("RW", [P, KD, NE])
        RB = sb("RB", [P, NE])
        mark, mk2 = sb("mark", [P, 1]), sb("mk2", [P, 1])
        zeros = page(49.75, 256)
        route = page(41, 2048)

        def cut(at, *shape):
            v = route[:, at:at + math.prod(shape)]
            return v if len(shape) == 1 else v.rearrange("p (a b) -> p a b", a=shape[0]) if len(shape) == 2 \
                else v.rearrange("p (a b c) -> p a b c", a=shape[0], b=shape[1])

        score, biased, chosen, weighted = (cut(80 * i, NT, NE) for i in range(4))
        above, equal = cut(320, NT * NG, EG, EG), cut(640, NT * NG, EG, EG)
        place, spot, mine = (cut(960 + 80 * i, NT, NE) for i in range(3))
        gsum, gtop = cut(1200, NT, NG), cut(1220, NT, NG)
        count, tiles_of, upto, base = (cut(1240 + 16 * i, NE) for i in range(4))
        wsum, tot = cut(1304, NT), cut(1312, NT)
        steps = cut(1320, MAXT)
        full = cut(1360, NE, NT)
        ended = cut(1440, MAXT, NE)
        gate2 = sb("gate2", [P, 2, NT])
        slotf = sb("slotf", [P, 2, NT])
        sloti = sb("sloti", [P, 2, NT], U32)
        eotf, eoti = sb("eotf", [1, MAXT]), sb("eoti", [1, MAXT], I32)
        npf, npi = sb("npf", [1, 1]), sb("npi", [1, 2], I32)
        XG = [page(43 + i, D) for i in range(2)]
        XGT = [page(45 + i, D).rearrange("p (k n) -> p k n", k=KD) for i in range(2)]
        YO = [page(47 + i, D) for i in range(2)]
        SG_, AC, AT = ([page(39 + 0.75 * i + 0.25 * j, FF) for i in range(2)] for j in range(3))
        WD = [page(18 + 2 * i, 2 * D).rearrange("p (k n) -> p k n", k=2) for i in range(2)]
        GY = [[page(34 + 2 * i + j, D) for j in range(2)] for i in range(2)]
        xs_d = nc.dram_tensor("slot_rows", (MAXT * P, D), F32, kind="Internal").ap()

        Y = page(34, NT * DI).rearrange("p (t n) -> p t n", t=NT)
        XT = page(44, NT * 512).rearrange("p (t n) -> p t n", t=NT)
        BT, CT = page(46.5, TOK), page(47.125, TOK)
        BK = page(47.75, NT * P).rearrange("p (t n) -> p t n", t=NT)
        CB = page(48.375, 2 * P).rearrange("p (d n) -> p d n", d=2)
        DTA, DA, EA, DTD = (page(48.625, 4 * 320)[:, 320 * i:320 * (i + 1)].rearrange("p (t d h) -> p t d h", t=NT, d=2)
                            for i in range(4))
        RR = page(28, 2048).rearrange("p (d h n) -> p d h n", d=2, h=HG)
        EE = page(30, 2048).rearrange("p (d h n) -> p d h n", d=2, h=HG)
        XS = page(32, 1024).rearrange("p (d h n) -> p d h n", d=2, h=HG)
        XD = page(33, 1024).rearrange("p (d h n) -> p d h n", d=2, h=HG)
        PV = page(18, 4096).rearrange("p (d c n) -> p d c n", d=2, c=NT - 1)
        UW = 2 + DEC + 2 + SEQ + 2
        AW = UW - 4
        U, AC2, CVT = ([page(22, 4096)[:, 650 * (2 * a + i):650 * (2 * a + i) + w] for i in range(2)]
                       for a, w in ((0, UW), (1, AW), (2, TOK)))
        RAW = page(16, 1024).rearrange("p (d a n) -> p d a n", d=2, a=4)
        TMP = page(17, 512)
        CW = page(17.5, 144).rearrange("p (c j) -> p c j", j=6)
        DROW = page(17.5, 512)[:, 144:144 + SH]
        CD = page(17.5, 512)[:, 176:176 + 320].rearrange("p (t d h) -> p t d h", t=NT, d=2)
        WX = WS[0]
        WBC = page(14, 2048).rearrange("p (k n) -> p k n", k=KD)
        WDT = page(33, 512).rearrange("p (k n) -> p k n", k=KD)
        CWR = page(28, 3072, 6)
        DTB, AROW = page(32, 64), page(32, 128)[:, 64:128]
        sp0, sp1, sp2, sp3, sp4 = (page(28, 5 * 320)[:, 320 * i:320 * (i + 1)].rearrange("p (t d h) -> p t d h", t=NT, d=2)
                                   for i in range(5))
        NGR = page(28, DI)
        ZS = [page(30 + 0.5 * i, 512) for i in range(2)]
        YQ = [page(31 + 0.5 * i, 512) for i in range(2)]
        ssy = sb("ssy", [P, NT, 4])
        ry = sb("ry", [P, NT])
        YT = [HT, page(44, KD * TOK).rearrange("p (k n) -> p k n", k=KD)]
        OM = [page(22 + 0.5 * i, 512) for i in range(2)]

        s_init, s_x = sem("s_init"), sem("s_x")
        s_condT, s_condS = sem("s_condT"), sem("s_condS")
        s_w = sems("s_w", 3)
        s_wused = sems("s_wused", 3)
        s_modfree = sems("s_modfree", 3)
        s_modst = sems("s_modst", 4)
        s_mb = sems("s_mb", 4)
        o_dve, o_act, o_pool = sem("o_dve"), sem("o_act"), sem("o_pool")
        s_amod = sem("s_amod")
        s_ss, s_var, s_sd = sem("s_ss"), sem("s_var"), sem("s_sd")
        s_hm, s_h, s_ht, s_hT = sem("s_hm"), sem("s_h"), sem("s_ht"), sem("s_hT")
        s_gqk, s_kv = sem("s_gqk"), sem("s_kv")
        s_qkv, s_sq, s_v, s_varq, s_sdq, s_qn, s_qg, s_t2, s_qf, s_tq, s_tqe = (
            sem(n) for n in "s_qkv s_sq s_v s_varq s_sdq s_qn s_qg s_t2 s_qf s_tq s_tqe".split())
        s_S, s_max, s_exp, s_T, s_pte, s_pv, s_oev, s_qc = (
            sem(n) for n in "s_S s_max s_exp s_T s_pte s_pv s_oev s_qc".split())
        s_ot, s_otT, s_op, s_opm, s_x1 = (sem(n) for n in "s_ot s_otT s_op s_opm s_x1".split())
        o_rden = sem("o_rden")
        o_u, o_cv, o_pv, o_y = sem("o_u"), sem("o_cv"), sem("o_pv"), sem("o_y")

        s_rw, s_zero, s_clear = sem("s_rw"), sem("s_zero"), sem("s_clear")

        s_ssdin, s_pre_pe, s_pre_act, s_pre_dve = (sem(n) for n in "s_ssdin s_pre_pe s_pre_act s_pre_dve".split())
        (s_wx, s_wbc, s_raw, s_ip, s_u, s_c0, s_cv, s_sl, s_tx, s_txe, s_rt, s_rte, s_xsd, s_st, s_ste, s_fs, s_cb,
         s_cbm, s_R, s_seg, s_E, s_M, s_xs, s_yd, s_yo, s_y, s_D, s_pad) = (sem(n) for n in (
            "s_wx s_wbc s_raw s_ip s_u s_c0 s_cv s_sl s_tx s_txe s_rt s_rte s_xsd s_st s_ste s_fs s_cb "
            "s_cbm s_R s_seg s_E s_M s_xs s_yd s_yo s_y s_D s_pad").split())
        s_fso = sems("s_fso", 2)
        s_z, s_zs, s_yz, s_yq, s_yg, s_ngr, s_sy, s_ryv, s_ryd, s_yt, s_yte = (
            sem(n) for n in "s_z s_zs s_yz s_yq s_yg s_ngr s_sy s_ryv s_ryd s_yt s_yte".split())
        s_op2, s_om, s_xadd, s_out = sem("s_op2"), sem("s_om"), sem("s_xadd"), sem("s_out")
        UNITS = [(0, 1), (1, 4), (0, 2), (1, 3), (0, 3), (1, 2), (0, 0), (1, 0)]
        MASK = [T_UP, T_LOW]
        PAST_ = [T_GT, T_LT]

        def moe_sems():
            names = "logit score sel pos slot sc xt xtc gu silu act at atc dn ycopy np all".split()
            m = {n: sem(f"s_e_{n}") for n in names}
            for n in "lgu ldn lxg yst gat".split():
                m[n] = sems(f"s_e_{n}", 2)
            m["x2"], m["wa"], m["wg"] = sem("s_x2"), sem("s_wa"), sem("s_wg")
            return m

        ES = moe_sems()

        W_BEFORE = [10, 10, 9]

        LED = {"pe": s_wused + [s_ip, s_seg, s_yd, ES["xt"], ES["gu"], ES["dn"], ES["at"]],
               "act": [s_E, ES["atc"], ES["ycopy"]] + s_fso + ES["yst"],
               "dve": s_modfree + [s_y, s_cbm, s_M],
               "pool": [s_D]}

        block = ctx.enter_context(nc.Block())

        @block.sync
        def _(sp):
            sp.dma_start(tab[:, :], consts).then_inc(s_init, 16)
            sp.dma_start(condr[0:8, :], c_ctx.rearrange("(k p) -> k p", p=P)).then_inc(s_init, 16)
            sp.dma_start(condr[8:16, :], c[0, :].rearrange("(k p) -> k p", p=P)).then_inc(s_init, 16)
            sp.dma_start(MR[0:1, :, :], mod_b.rearrange("(a l) n -> a l n", a=1)).then_inc(s_init, 16)
            sp.dma_start(MR[1:2, :, :], mod_b.rearrange("(a l) n -> a l n", a=1)).then_inc(s_init, 16)
            for l in range(2):
                wv = mod_w[l].rearrange("(k p) (i j n) -> j i p k n", p=P, j=3, n=512)
                with sp.Fori(0, 4) as i:
                    for j in range(3):
                        sp.wait_ge(s_wused[j], i + 4 * l + 1)
                        sp.dma_start(WS[j], wv[j, i]).then_inc(s_w[j], 16)
                if l == 0:
                    sp.dma_start(X[:, 0, :], x_prompt[0]).then_inc(s_x, 16)
                    sp.dma_start(X[:, 1:NT, :], x_sample[0].rearrange("(t p) n -> p t n", p=P)).then_inc(s_x, 16)
            for j in range(3):
                sp.wait_ge(s_wused[j], 9)
                sp.dma_start(WS[j], w_qkv[0].rearrange("(k p) (j n) -> j p k n", p=P, j=3)[j]).then_inc(s_w[j], 16)
            sp.dma_start(gqk[:, 0, :], q_g.partition_broadcast(P)).then_inc(s_gqk, 16)
            sp.dma_start(gqk[:, 1, :], k_g.partition_broadcast(P)).then_inc(s_gqk, 16)
            sp.wait_ge(s_qkv, NT)
            for j in range(2):
                sp.dma_start(WS[j], w_o[0].rearrange("(k p) (j n) -> j p k n", p=P, j=2)[j]).then_inc(s_w[j], 16)

            sp.wait_ge(s_zero, 1)
            sp.dma_start(xs_d.rearrange("(p a) (b n) -> p (a b) n", p=P, n=256),
                         zeros.unsqueeze(1).to_broadcast([P, MAXT * 4, 256])).then_inc(s_clear, 16)
            sp.dma_start(RW[:, :, :], router_w.rearrange("(k p) e -> p k e", p=P)).then_inc(s_rw, 16)
            sp.dma_start(RB[:, :], router_b.partition_broadcast(P)).then_inc(s_rw, 16)

            def expert_loads(l):
                sp.wait_ge(ES["np"], l + 1)
                done = 0 if l == 0 else sp.value_load(npi[0:1, 0:1], min_val=1, max_val=MAXT // 2)
                pairs = sp.value_load(npi[0:1, l:l + 1], min_val=1, max_val=MAXT // 2)
                sp.wait_ge(ES["sc"], 2 * NT * 16 * (l + 1))
                if l == 0:
                    sp.wait_ge(s_op, NT)
                with sp.Fori(0, pairs) as i:
                    turn = i + done
                    for j in range(2):
                        e = sp.value_load(eoti[0:1, bass.ds(i * 2 + j, 1)], min_val=0, max_val=NE - 1)
                        sp.wait_ge(ES["xt"], turn * 2 + j + 1)
                        sp.dma_start(XG[j], xs_d.rearrange("(a p) n -> a p n", p=P)[i * 2 + j]).then_inc(ES["lxg"][j], 16)
                        if j == 0:
                            sp.wait_ge(ES["gu"], turn * 2 + 1)
                        else:
                            sp.wait_ge(ES["gu"], turn * 2 + 1)
                        gv = w_gate[l].rearrange("e (k p) f -> e p k f", p=P)
                        uv = w_up[l].rearrange("e (k p) f -> e p k f", p=P)
                        dv = w_down[l].rearrange("e (k p) n -> e p k n", p=P)
                        sp.dma_start(WS[j][:, :, 0:FF], gv[e]).then_inc(ES["lgu"][j], 16)
                        sp.dma_start(WS[j][:, :, FF:2 * FF], uv[e]).then_inc(ES["lgu"][j], 16)
                        sp.wait_ge(ES["dn"], turn * 2 + 1)
                        sp.dma_start(WD[j], dv[e]).then_inc(ES["ldn"][j], 16)

            expert_loads(0)

            ipv = in_proj[0].rearrange("(k p) n -> p k n", p=P)
            sp.wait_ge(s_ht, 3 * NT)
            sp.dma_start(CWR[0:5, :], conv_w[0]).then_inc(s_ssdin, 16)
            sp.dma_start(CWR[5:6, :], conv_b).then_inc(s_ssdin, 16)
            sp.dma_start(WDT, ipv[:, :, 2 * DI + 2 * SG * SN:2 * DI + 2 * SG * SN + 2 * SH]).then_inc(s_ssdin, 16)
            sp.dma_start(DTB, dt_bias[0].rearrange("d h -> (d h)").partition_broadcast(P)).then_inc(s_ssdin, 16)
            sp.dma_start(AROW, a_log[0].rearrange("d h -> (d h)").partition_broadcast(P)).then_inc(s_ssdin, 16)
            sp.dma_start(DROW, ssd_d[0].partition_broadcast(P)).then_inc(s_ssdin, 16)
            with sp.Fori(0, SG) as g:
                sp.wait_ge(s_ip, g * 6 + 1)
                sp.dma_start(WX, ipv[:, :, DI:2 * DI].rearrange("p k (g n) -> g p k n", g=SG)[g]).then_inc(s_wx, 16)
                for a in range(2):
                    sp.dma_start(WBC[:, :, a * P:(a + 1) * P],
                                 ipv[:, :, 2 * DI + a * SG * SN:2 * DI + (a + 1) * SG * SN]
                                 .rearrange("p k (g n) -> g p k n", g=SG)[g]).then_inc(s_wbc, 16)
                for d in range(2):
                    sp.wait_ge(s_fso[d], g * 16 + 1)
                    sp.dma_start(RAW[:, d], state_ssm[0, 0, d].rearrange("(g a b) q n -> g (b q) a n", g=SG, b=2)[g])\
                        .then_inc(s_raw, 16)
            zv = ipv[:, :, 0:DI].rearrange("p k (c n) -> c p k n", c=4)
            sp.wait_ge(s_ip, SG * 6 + 1)
            sp.wait_ge(s_fso[0], SG * 16 + 1)
            sp.wait_ge(s_fso[1], SG * 16 + 1)
            sp.dma_start(WS[0], zv[0]).then_inc(s_w[0], 16)
            sp.wait_ge(s_y, 5 * SG + 1)
            sp.dma_start(WS[1], zv[1]).then_inc(s_w[1], 16)
            sp.dma_start(WS[2], zv[2]).then_inc(s_w[2], 16)
            sp.dma_start(NGR, ssd_g[0].partition_broadcast(P)).then_inc(s_ngr, 16)
            sp.wait_ge(s_z, NT)
            sp.dma_start(WS[0], zv[3]).then_inc(s_w[0], 16)
            ov = out_proj[0].rearrange("(b k p) (a n) -> a b p k n", b=2, p=P, a=2)
            sp.wait_ge(s_z, 2 * NT)
            sp.dma_start(WS[1], ov[0, 0]).then_inc(s_w[1], 16)
            sp.wait_ge(s_z, 3 * NT)
            sp.dma_start(WS[2], ov[0, 1]).then_inc(s_w[2], 16)
            sp.wait_ge(s_z, 4 * NT)
            sp.dma_start(WS[0], ov[1, 0]).then_inc(s_w[0], 16)
            sp.wait_ge(s_op2, NT)
            sp.dma_start(WS[1], ov[1, 1]).then_inc(s_w[1], 16)
            sp.wait_ge(s_op2, 2 * NT)
            expert_loads(1)

        @block.tensor
        def _(pe):
            for s in LED["pe"]:
                pe.sem_inc(s, 1)
            def norm_transposes(nn):
                for t in range(NT):
                    n = nn * NT + t
                    pe.wait_ge(s_h, n + 1)
                    if n >= 2:
                        pe.wait_ge(s_hT, n - 1)
                    for k in range(KD):
                        last = nc.tensor.transpose(psf[:, (n % 2) * 1024 + k * P:(n % 2) * 1024 + (k + 1) * P],
                                                   H[:, t, k * P:(k + 1) * P], ident)
                    last.then_inc(s_ht, 1)

            pe.wait_ge(s_init, 80)
            nc.tensor.transpose(ps[:, 7, 0:16], condr[0:16, :], ident[0:16, 0:16]).then_inc(s_condT, 1)
            pe.wait_ge(s_condS, 1)
            for l in range(2):
                with pe.Fori(0, 4) as i:
                    for j in range(3):
                        pe.wait_ge(s_w[j], (i + (4 * l + 1)) * 16)
                        pe.wait_ge(s_modfree[j], i + 4 * l + 1)
                        for k in range(KD):
                            last = nc.tensor.matmul(ps[0:2, j, :], condT[:, :, k], WS[j][:, k, :],
                                                    start=(k == 0), stop=(k == KD - 1))
                        last.then_inc(s_wused[j], 1)
            for j in range(3):
                pe.wait_ge(s_modfree[j], 9)
            norm_transposes(0)

            def turn_heads(t):
                src = [QF[:, 0:512], QF[:, 512:1024], KDUP[:, :, :, :].rearrange("p g two d -> p (g two d)")]
                if t == NT:
                    pe.wait_ge(s_kv, 48)
                    src = [KDC[:, :, :, :].rearrange("p g two d -> p (g two d)")]
                else:
                    pe.wait_ge(s_qf, t + 1)
                for r, s in enumerate(src):
                    m = 3 * t + r
                    if m >= 2:
                        pe.wait_ge(s_tqe, m - 1)
                    for a in range(4):
                        last = nc.tensor.transpose(ps[:, 6 + m % 2, a * P:(a + 1) * P], s[:, a * P:(a + 1) * P], ident)
                    last.then_inc(s_tq, 1)

            for j in range(3):
                pe.wait_ge(s_w[j], 9 * 16)
            for t in range(NT):
                pe.wait_ge(s_hT, t + 1)
                if t == 0:
                    pe.wait_ge(s_hT, 5)
                if t >= 2:
                    pe.wait_ge(s_qn, t - 1)
                    pe.wait_ge(s_v, t - 1)
                for j in range(3):
                    for k in range(KD):
                        last = nc.tensor.matmul(ps[:, 3 * (t % 2) + j, :], HT[:, k, t * P:(t + 1) * P], WS[j][:, k, :],
                                                start=(k == 0), stop=(k == KD - 1))
                last.then_inc(s_qkv, 1)
                if t >= 1:
                    turn_heads(t - 1)
            turn_heads(NT - 1)
            turn_heads(NT)

            def attend(T, k0, nk):
                def scores(h):
                    u = T * NH + h
                    b, half = h % 2, h % 2
                    if h == 0:
                        pe.wait_ge(s_qc, T + 1)
                    if not (isinstance(T, int) and T == 0 and h < 2):
                        pe.wait_ge(s_exp, u - 1)
                    q = QC[64 * half:64 * half + 64, h // 2, :]
                    kk = KT[64 * half:64 * half + 64, h // 4, :]
                    n = min(nk, 4) * P
                    last = nc.tensor.matmul(ps[:, 2 * b, 0:n], q, kk[:, k0 * P:k0 * P + n], start=True, stop=True)
                    if nk > 4:
                        last = nc.tensor.matmul(ps[:, 2 * b + 1, 0:P], q, kk[:, k0 * P + n:k0 * P + n + P],
                                                start=True, stop=True)
                    last.then_inc(s_S, 1)

                def turn(h):
                    u = T * NH + h
                    pe.wait_ge(s_exp, u + 1)
                    if not (isinstance(T, int) and T == 0 and h == 0):
                        pe.wait_ge(s_pte, u)
                    for j in range(nk):
                        last = nc.tensor.transpose(psf[:, 2048 + j * P:2048 + (j + 1) * P],
                                                   PR[h % 2][:, j * P:(j + 1) * P], ident)
                    last.then_inc(s_T, 1)

                def values(h):
                    u = T * NH + h
                    if h % 8 == 0 and not (isinstance(T, int) and T == 0):
                        pe.wait_ge(s_oev, 2 * T - 1 + h // 8)
                    pe.wait_ge(s_pte, u + 1)
                    for j in range(nk):
                        last = nc.tensor.matmul(ps[:, 6 + h // 8, (h % 8) * HD:(h % 8 + 1) * HD],
                                                PT[h % 2][:, j * P:(j + 1) * P],
                                                V[:, k0 + j, (h // 4) * HD:(h // 4 + 1) * HD],
                                                start=(j == 0), stop=(j == nk - 1))
                    last.then_inc(s_pv, 1)

                for s in range(NH + 2):
                    if s < NH:
                        scores(s)
                    if 1 <= s <= NH:
                        turn(s - 1)
                    if s >= 2:
                        values(s - 2)

            pe.wait_ge(s_tqe, 16)
            pe.wait_ge(s_qn, NT)
            pe.wait_ge(s_v, NT)
            attend(0, 0, 1)
            with pe.Fori(0, NT - 1) as i:
                attend(i + 1, 1, 5)

            pe.wait_ge(s_w[0], 160)
            pe.wait_ge(s_w[1], 160)
            pe.wait_ge(s_oev, 10)
            for s in range(NT + 1):
                if s < NT:
                    t = s
                    if t >= 2:
                        pe.wait_ge(s_otT, t - 1)
                    for k in range(KD):
                        last = nc.tensor.transpose(psf[:, (t % 2) * 1024 + k * P:(t % 2) * 1024 + (k + 1) * P],
                                                   OA[:, t, k * P:(k + 1) * P], ident)
                    last.then_inc(s_ot, 1)
                if s >= 1:
                    t = s - 1
                    pe.wait_ge(s_otT, t + 1)
                    if t >= 2:
                        pe.wait_ge(s_opm, t - 1)
                    for j in range(2):
                        for k in range(KD):
                            last = nc.tensor.matmul(ps[:, 4 + 2 * (t % 2) + j, :], HT[:, k, t * P:(t + 1) * P],
                                                    WS[j][:, k, :], start=(k == 0), stop=(k == KD - 1))
                    last.then_inc(s_op, 1)

            def moe(l):
                nn = 2 * l + 1
                norm_transposes(nn)
                pe.wait_ge(s_rw, 32)
                for t in range(NT):
                    pe.wait_ge(s_hT, nn * NT + t + 1)
                    for k in range(KD):
                        last = nc.tensor.matmul(ps[:, 4, t * NE:(t + 1) * NE], HT[:, k, t * P:(t + 1) * P], RW[:, k, :],
                                                start=(k == 0), stop=(k == KD - 1))
                last.then_inc(ES["logit"], 1)
                pe.wait_ge(ES["sel"], l + 1)
                ones = tab[:, T_ONE:T_ONE + P]
                before = tab[:, T_LT:T_LT + P]
                for t in range(NT):
                    for a in range(t):
                        nc.tensor.matmul(ps[:, 5, t * NE:(t + 1) * NE], ones, chosen[:, a, :], start=(a == 0), stop=False)
                    nc.tensor.matmul(ps[:, 5, t * NE:(t + 1) * NE], before, chosen[:, t, :], start=(t == 0), stop=True)
                for t in range(NT):
                    last = nc.tensor.matmul(ps[:, 5, NT * NE:(NT + 1) * NE], ones, chosen[:, t, :], start=(t == 0), stop=(t == NT - 1))
                last.then_inc(ES["pos"], 1)

                pe.wait_ge(ES["np"], l + 1)
                done = 0 if l == 0 else pe.value_load(npi[0:1, 0:1], min_val=1, max_val=MAXT // 2)
                pairs = pe.value_load(npi[0:1, l:l + 1], min_val=1, max_val=MAXT // 2)
                pe.wait_ge(ES["slot"], l + 1)
                with pe.Fori(0, pairs) as i:
                    turn = i + done
                    for j in range(2):
                        pe.wait_ge(ES["lxg"][j], (turn + 1) * 16)
                        pe.wait_ge(ES["atc"], turn * 2 + 1)
                        for k in range(KD):
                            last = nc.tensor.transpose(psf[:, j * 1024 + k * P:j * 1024 + (k + 1) * P],
                                                       XG[j][:, k * P:(k + 1) * P], ident)
                        last.then_inc(ES["xt"], 1)
                    for j in range(2):
                        pe.wait_ge(ES["lgu"][j], (turn + 1) * 32)
                        pe.wait_ge(ES["xtc"], turn * 2 + j + 1)
                        pe.wait_ge(ES["ycopy"], turn * 2 + 1)
                        for k in range(KD):
                            last = nc.tensor.matmul(ps[:, 4 + j, :], XGT[j][:, k, :], WS[j][:, k, :],
                                                    start=(k == 0), stop=(k == KD - 1))
                        last.then_inc(ES["gu"], 1)
                    for j in range(2):
                        pe.wait_ge(ES["act"], turn * 2 + j + 1)
                        for k in range(2):
                            last = nc.tensor.transpose(psf[:, j * 1024 + k * P:j * 1024 + (k + 1) * P],
                                                       AC[j][:, k * P:(k + 1) * P], ident)
                        last.then_inc(ES["at"], 1)
                        pe.wait_ge(ES["atc"], turn * 2 + j + 2)
                        pe.wait_ge(ES["ldn"][j], (turn + 1) * 16)
                        if j == 1:
                            pe.wait_ge(ES["act"], turn * 2 + 2)
                        for n in range(2):
                            for k in range(2):
                                last = nc.tensor.matmul(ps[:, 6 - 2 * j + n, :], AT[j][:, k * P:(k + 1) * P], WD[j][:, k, n * 512:(n + 1) * 512],
                                                        start=(k == 0), stop=(k == 1))
                        last.then_inc(ES["dn"], 1)

            moe(0)
            norm_transposes(2)

            pe.wait_ge(s_ssdin, 96)
            for a in range(24):
                last = nc.tensor.transpose(ps[:, 7, a * 6:(a + 1) * 6], CWR[0:6, a * P:(a + 1) * P], ident[0:6, 0:6])
            last.then_inc(s_pre_pe, 1)
            pe.wait_ge(s_ssdin, 96)
            for t in range(NT):
                pe.wait_ge(s_hT, 2 * NT + t + 1)
                for k in range(KD):
                    last = nc.tensor.matmul(ps[:, 6, t * 64:(t + 1) * 64], HT[:, k, t * P:(t + 1) * P], WDT[:, k, :],
                                            start=(k == 0), stop=(k == KD - 1))
            last.then_inc(s_pre_pe, 1)
            pe.wait_ge(s_pre_dve, 3)
            pe.wait_ge(s_pre_act, 1)
            for d in range(2):
                for bank, m in ((4, MASK[d]), (5, PAST_[d])):
                    nc.tensor.matmul(ps[:, bank, 0:320].rearrange("p (t d h) -> p t d h", t=NT, d=2)[:, :, d, :],
                                     tab[:, m:m + P], DA[:, :, d, :], start=True, stop=True)
            nc.tensor.matmul(ps[:, 7, 0:320], tab[:, T_ONE:T_ONE + P], DA.rearrange("p t d h -> p (t d h)"),
                             start=True, stop=True).then_inc(s_pre_pe, 1)

            pe.wait_ge(s_pre_act, 7)
            with pe.Fori(0, SG) as g:
                pe.wait_ge(s_E, g * 5 + 1)
                pe.wait_ge(s_y, g * 5 + 1)
                pe.wait_ge(s_cbm, g * 5 + 1)
                for st in range(7):
                    if st < 6:
                        if st == 0:
                            pe.wait_ge(s_wx, (g + 1) * 16)
                        if st == 4:
                            pe.wait_ge(s_wbc, (g + 1) * 32)
                        if st >= 2:
                            pe.wait_ge(s_u, g * 6 + st - 1)
                        b = 2 * (st % 2)
                        w = WX[:, :, st * P:(st + 1) * P] if st < 4 else WBC[:, :, (st - 4) * P:(st - 3) * P]
                        for k in range(KD):
                            nc.tensor.matmul(ps[:, b, :], w[:, k, :], HT[:, k, SEQ:TOK], start=(k == 0), stop=(k == KD - 1))
                        for k in range(KD):
                            last = nc.tensor.matmul(ps[:, b + 1, 0:SEQ], w[:, k, :], HT[:, k, 0:SEQ],
                                                    start=(k == 0), stop=(k == KD - 1))
                        last.then_inc(s_ip, 1)
                    if 2 <= st:
                        a = st - 2
                        pe.wait_ge(s_sl, g * 6 + a + 1)
                        if a >= 1:
                            pe.wait_ge(s_txe, g * 5 + a)
                        src = CVT[a % 2] if a < 4 else BT
                        for t in range(NT):
                            last = nc.tensor.transpose(psf[:, 2048 + t * P:2048 + (t + 1) * P], src[:, t * P:(t + 1) * P], ident)
                        last.then_inc(s_tx, 1)
                pe.wait_ge(s_raw, (g + 1) * 32)
                for d in range(2):
                    for a in range(4):
                        last = nc.tensor.transpose(ps[:, 6 + d, a * P:(a + 1) * P], RAW[:, d, a, :], ident)
                    last.then_inc(s_rt, 1)
                pe.wait_ge(s_txe, (g + 1) * 5)
                for i, (d, cc) in enumerate(UNITS):
                    pe.wait_ge(s_xsd, g * 8 + i + 1)
                    if 2 <= i:
                        pe.wait_ge(s_ste, g * 6 + min(i - 1, 6))
                    xd = XD[:, d].rearrange("p h n -> p (h n)")
                    if cc > 0:
                        last = nc.tensor.matmul(ps[:, 4 + i % 2, :], BK[:, cc, :], xd, start=True, stop=True)
                    else:
                        for a in range(4):
                            last = nc.tensor.matmul(ps[:, 4 + i % 2, a * P:(a + 1) * P], xd[:, a * P:(a + 1) * P],
                                                    BK[:, 0, :], start=True, stop=True)
                    last.then_inc(s_st, 1)

                def decay_and_cb(cc):
                    if cc >= 1:
                        pe.wait_ge(s_cbm, g * 5 + cc + 1)
                        pe.wait_ge(s_E, g * 5 + cc + 1)
                    nc.tensor.matmul(ps[:, 5, 0:P], BT[:, cc * P:(cc + 1) * P], CT[:, cc * P:(cc + 1) * P],
                                     start=True, stop=True).then_inc(s_cb, 1)
                    pe.wait_ge(s_R, g * 5 + cc + 1)
                    for d in range(2):
                        for h in range(2):
                            last = nc.tensor.matmul(ps[:, 2 * d + h, :], tab[:, PAST_[d]:PAST_[d] + P],
                                                    RR[:, d, 4 * h:4 * h + 4, :].rearrange("p h n -> p (h n)"),
                                                    start=True, stop=True)
                    last.then_inc(s_seg, 1)

                pe.wait_ge(s_u, (g + 1) * 6)
                pe.wait_ge(s_sl, (g + 1) * 6)
                pe.wait_ge(s_fs, (g + 1) * 2)
                decay_and_cb(0)
                for cc in range(NT):
                    if cc + 1 < NT:
                        decay_and_cb(cc + 1)
                    if cc >= 1:
                        pe.wait_ge(s_y, g * 5 + cc + 1)
                        if cc == 1:
                            pe.wait_ge(s_rte, (g + 1) * 2)
                            pe.wait_ge(s_ste, (g + 1) * 6)
                        for d in range(2):
                            last = nc.tensor.matmul(ps[:, 6 + d, :], CT[:, cc * P:(cc + 1) * P], PV[:, d, cc - 1, :],
                                                    start=True, stop=True)
                        last.then_inc(s_yo, 1)
                    pe.wait_ge(s_xs, g * 5 + cc + 1)
                    pe.wait_ge(s_M, g * 5 + cc + 2)
                    for h in range(HG):
                        for d in range(2):
                            last = nc.tensor.matmul(ps[:, 4, h * SP:(h + 1) * SP], EE[:, d, h, :], XS[:, d, h, :],
                                                    start=(d == 0), stop=(d == 1))
                    last.then_inc(s_yd, 1)

            pe.wait_ge(s_E, SG * 5 + 1)
            for j in range(4):
                pe.wait_ge(s_w[j % 3], 16 * (W_BEFORE[j % 3] + j // 3 + 1))
                for t in range(NT):
                    n = j * NT + t
                    if n >= 4:
                        pe.wait_ge(s_zs, n - 3)
                    for k in range(KD):
                        last = nc.tensor.matmul(ps[:, n % 4, :], HT[:, k, t * P:(t + 1) * P], WS[j % 3][:, k, :],
                                                start=(k == 0), stop=(k == KD - 1))
                    last.then_inc(s_z, 1)
            pe.wait_ge(s_zs, 4 * NT)
            for t in range(NT):
                for b in range(2):
                    n = 2 * t + b
                    pe.wait_ge(s_yg, 3 * NT + t + 1)
                    if n >= 2:
                        pe.wait_ge(s_yte, n - 1)
                    for k in range(KD):
                        last = nc.tensor.transpose(psf[:, b * 1024 + k * P:b * 1024 + (k + 1) * P],
                                                   Y[:, t, (b * KD + k) * P:(b * KD + k + 1) * P], ident)
                    last.then_inc(s_yt, 1)
            for a in range(2):
                for b in range(2):
                    i = (1 + 2 * a + b) % 3
                    pe.wait_ge(s_w[i], 16 * (W_BEFORE[i] + (3 if (a, b) != (0, 0) and i != 2 else 2)))
                for t in range(NT):
                    n = a * NT + t
                    pe.wait_ge(s_yte, 2 * t + 2)
                    if n >= 4:
                        pe.wait_ge(s_om, n - 3)
                    if n == 0:
                        pe.wait_ge(s_y, SG * 5 + 1)
                    for b in range(2):
                        w = WS[(1 + 2 * a + b) % 3]
                        for k in range(KD):
                            last = nc.tensor.matmul(ps[:, 4 + n % 4, :], YT[b][:, k, t * P:(t + 1) * P], w[:, k, :],
                                                    start=(b == 0 and k == 0), stop=(b == 1 and k == KD - 1))
                    last.then_inc(s_op2, 1)
            moe(1)

        @block.scalar
        def _(act):
            for s in LED["act"]:
                act.sem_inc(s, 1)
            order = Order(act, o_act)

            def norm_squares(nn):
                for t in range(NT):
                    if nn == 0:
                        act.wait_ge(s_x, 32)
                    order(nc.scalar.activation(SQX, X[:, t, :], ACT.Square, accum_out=ssq[:, t:t + 1]))
                nc.scalar.activation(ssq[:, 5:6], ssq[:, 0:1], ACT.Copy).then_inc(s_ss, 1)
                act.wait_ge(s_var, nn + 1)
                nc.scalar.activation(ssq[:, 0:NT], ssq[:, 0:NT], ACT.Sqrt).then_inc(s_sd, 1)

            def norm_columns(nn):
                for t in range(NT):
                    n = nn * NT + t
                    act.wait_ge(s_ht, n + 1)
                    nc.scalar.activation(HT[:, :, t * P:(t + 1) * P],
                                         psf[:, (n % 2) * 1024:(n % 2) * 1024 + 1024].rearrange("p (k n) -> p k n", k=KD),
                                         ACT.Copy).then_inc(s_hT, 1)

            act.wait_ge(s_condT, 1)
            nc.scalar.activation(condT[:, :, :].rearrange("p c k -> p (c k)"), ps[:, 7, 0:16], ACT.Silu).then_inc(s_condS, 1)
            for j in range(3):
                act.wait_ge(s_modfree[j], 9)
            act.wait_ge(s_modst[0], 16)
            act.wait_ge(s_modst[1], 16)
            act.wait_ge(s_modst[2], 16)
            act.wait_ge(s_modst[3], 16)
            norm_squares(0)
            norm_columns(0)

            def head_columns(t):
                dst = [QT[:, 0:4, t * P:(t + 1) * P], QT[:, 4:8, t * P:(t + 1) * P], KT[:, :, t * P:(t + 1) * P]] \
                    if t < NT else [KT[:, :, t * P:(t + 1) * P]]
                for r, d in enumerate(dst):
                    m = 3 * t + r
                    act.wait_ge(s_tq, m + 1)
                    nc.scalar.activation(d, ps[:, 6 + m % 2, :].rearrange("p (a n) -> p a n", a=4), ACT.Copy)\
                        .then_inc(s_tqe, 1)

            for t in range(NT):
                b = 3 * (t % 2) * 512
                act.wait_ge(s_qkv, t + 1)
                nc.scalar.activation(SQ, psf[:, b:b + QK], ACT.Square).then_inc(s_sq, 1)
                nc.scalar.activation(V[:, t, :], psf[:, b + QK:b + QK + 256], ACT.Copy).then_inc(s_v, 1)
                act.wait_ge(s_varq, t + 1)
                nc.scalar.activation(rs[:, :], rs[:, :], ACT.Sqrt).then_inc(s_sdq, 1)
                if t >= 1:
                    head_columns(t - 1)
            head_columns(NT - 1)
            head_columns(NT)

            def probabilities(T, nk):
                for h in range(NH):
                    u = T * NH + h
                    act.wait_ge(s_max, u + 1)
                    if not (isinstance(T, int) and T == 0 and h < 2):
                        act.wait_ge(s_T, u - 1)
                    nc.scalar.activation(PR[h % 2][:, 0:nk * P], psf[:, 1024 * (h % 2):1024 * (h % 2) + nk * P],
                                         ACT.Exp, bias=nmx[:, h:h + 1], accum_out=den[:, h:h + 1]).then_inc(s_exp, 1)

            probabilities(0, 1)
            with act.Fori(0, NT - 1) as i:
                probabilities(i + 1, 5)

            for t in range(NT):
                act.wait_ge(s_ot, t + 1)
                nc.scalar.activation(HT[:, :, t * P:(t + 1) * P],
                                     psf[:, (t % 2) * 1024:(t % 2) * 1024 + 1024].rearrange("p (k n) -> p k n", k=KD),
                                     ACT.Copy).then_inc(s_otT, 1)

            def moe(l):
                nn = 2 * l + 1
                for t in range(NT):
                    act.wait_ge(s_x1, l * NT + t + 1)
                    order(nc.scalar.activation(SQX, X[:, t, :], ACT.Square, accum_out=ssq[:, t:t + 1]))
                nc.scalar.activation(ssq[:, 5:6], ssq[:, 0:1], ACT.Copy).then_inc(s_ss, 1)
                act.wait_ge(s_var, nn + 1)
                nc.scalar.activation(ssq[:, 0:NT], ssq[:, 0:NT], ACT.Sqrt).then_inc(s_sd, 1)
                norm_columns(nn)
                act.wait_ge(ES["logit"], l + 1)
                nc.scalar.activation(score, ps[:, 4, 0:NT * NE].rearrange("p (t e) -> p t e", t=NT), ACT.Sigmoid)\
                    .then_inc(ES["score"], 1)
                act.wait_ge(ES["np"], l + 1)
                done = 0 if l == 0 else act.value_load(npi[0:1, 0:1], min_val=1, max_val=MAXT // 2)
                pairs = act.value_load(npi[0:1, l:l + 1], min_val=1, max_val=MAXT // 2)
                with act.Fori(0, pairs) as i:
                    turn = i + done
                    for j in range(2):
                        act.wait_ge(ES["xt"], turn * 2 + j + 2)
                        nc.scalar.activation(XGT[j], psf[:, j * 1024:(j + 1) * 1024].rearrange("p (k n) -> p k n", k=KD),
                                             ACT.Copy).then_inc(ES["xtc"], 1)
                    for j in range(2):
                        act.wait_ge(ES["gu"], turn * 2 + j + 2)
                        nc.scalar.activation(SG_[j], ps[:, 4 + j, 0:FF], ACT.Silu).then_inc(ES["silu"], 1)
                    for j in range(2):
                        act.wait_ge(ES["at"], turn * 2 + j + 2)
                        nc.scalar.activation(AT[j], psf[:, j * 1024:j * 1024 + FF], ACT.Copy).then_inc(ES["atc"], 1)
                    for j in range(2):
                        act.wait_ge(ES["dn"], turn * 2 + j + 2)
                        act.wait_ge(ES["yst"][j], turn * 16 + 1)
                        nc.scalar.activation(YO[j], psf[:, (6 - 2 * j) * 512:(6 - 2 * j) * 512 + D], ACT.Copy)\
                            .then_inc(ES["ycopy"], 1)
                        act.wait_ge(ES["ycopy"], turn * 2 + j + 2)
                        act.dma_start(xs_d.rearrange("(a p) n -> a p n", p=P)[i * 2 + j], YO[j]).then_inc(ES["yst"][j], 16)
                for t in range(NT):
                    act.wait_ge(ES["gat"][t % 2], 32 * (t // 2 + 1 + l * (3 - t % 2)))
                    nc.scalar.activation(GY[t % 2][0], GY[t % 2][0], ACT.Copy, scale=gate2[:, 0, t:t + 1]).then_inc(ES["wa"], 1)

            moe(0)
            for t in range(NT):
                act.wait_ge(ES["x2"], t + 1)
                order(nc.scalar.activation(SQX, X[:, t, :], ACT.Square, accum_out=ssq[:, t:t + 1]))
            nc.scalar.activation(ssq[:, 5:6], ssq[:, 0:1], ACT.Copy).then_inc(s_ss, 1)
            act.wait_ge(s_var, 3)
            nc.scalar.activation(ssq[:, 0:NT], ssq[:, 0:NT], ACT.Sqrt).then_inc(s_sd, 1)
            norm_columns(2)

            act.wait_ge(s_pre_pe, 1)
            nc.scalar.activation(CW, ps[:, 7, 0:144].rearrange("p (c j) -> p c j", j=6), ACT.Copy).then_inc(s_pre_act, 1)
            act.wait_ge(s_pre_dve, 1)
            nc.scalar.activation(sp1, sp1, ACT.Exp).then_inc(s_pre_act, 1)
            act.wait_ge(s_ssdin, 96)
            nc.scalar.activation(AROW, AROW, ACT.Exp).then_inc(s_pre_act, 1)
            act.wait_ge(s_pre_dve, 2)
            nc.scalar.activation(sp3, sp2, ACT.Ln).then_inc(s_pre_act, 1)
            act.wait_ge(s_pre_pe, 3)
            for i, dst in enumerate((EA, sp0, CD)):
                nc.scalar.activation(dst, ps[:, (4, 5, 7)[i], 0:320].rearrange("p (t d h) -> p t d h", t=NT, d=2),
                                     ACT.Exp).then_inc(s_pre_act, 1)
            act.wait_ge(s_pad, 1)
            with act.Fori(0, SG) as g:
                act.wait_ge(s_D, g * 5 + 1)
                for st in range(8):
                    if st < 6:
                        b = 1024 * (st % 2)
                        act.wait_ge(s_ip, g * 6 + st + 2)
                        nc.scalar.activation(U[st % 2][:, 2:2 + DEC], psf[:, b:b + DEC], ACT.Copy).then_inc(o_u, 1)
                        nc.scalar.activation(U[st % 2][:, 4 + DEC:4 + DEC + SEQ], psf[:, b + 512:b + 512 + SEQ], ACT.Copy)\
                            .then_inc(s_u, 1)
                        act.wait_ge(s_u, g * 6 + st + 1)
                        act.wait_ge(o_u, g * 6 + st + 1)
                        ch = (g * 4 + st) if st < 4 else (g + 16 + 4 * (st - 4))
                        nc.scalar.activation(AC2[st % 2], U[st % 2][:, 2:2 + AW], ACT.Identity,
                                             scale=CW[:, bass.ds(ch, 1), 2:3].rearrange("p a b -> p (a b)"),
                                             bias=CW[:, bass.ds(ch, 1), 5:6].rearrange("p a b -> p (a b)")).then_inc(s_c0, 1)
                    if 1 <= st <= 6:
                        a = st - 1
                        act.wait_ge(s_cv, g * 6 + a + 1)
                        if 2 <= a < 4:
                            act.wait_ge(s_tx, g * 5 + a - 1)
                        dst = CVT[a % 2] if a < 4 else (BT if a == 4 else CT)
                        nc.scalar.activation(dst[:, SEQ:TOK], AC2[a % 2][:, 0:DEC], ACT.Silu)
                        nc.scalar.activation(dst[:, 0:SEQ], AC2[a % 2][:, DEC + 2:DEC + 2 + SEQ], ACT.Silu).then_inc(s_sl, 1)
                    if 3 <= st:
                        a = st - 3
                        act.wait_ge(s_tx, g * 5 + a + 1)
                        dst = XT[:, :, a * P:(a + 1) * P] if a < 4 else BK
                        nc.scalar.activation(dst, psf[:, 2048:2048 + TOK].rearrange("p (t n) -> p t n", t=NT), ACT.Copy)\
                            .then_inc(s_txe, 1)
                for d in range(2):
                    act.wait_ge(s_rt, g * 2 + d + 1)
                    nc.scalar.activation(PV[:, d, 3 * d, :], ps[:, 6 + d, :], ACT.Copy).then_inc(s_rte, 1)
                for d in range(2):
                    act.wait_ge(s_st, g * 8 + 7 + d)
                    nc.scalar.activation(RAW[:, d].rearrange("p a n -> p (a n)"), ps[:, 4 + d, :], ACT.Copy).then_inc(s_fs, 1)
                for d in range(2):
                    act.wait_ge(s_fs, g * 2 + 1 + d)
                    act.dma_start(new_ssm[0, 0, d].rearrange("(g a b) q n -> g (b q) a n", g=SG, b=2)[g], RAW[:, d])\
                        .then_inc(s_fso[d], 16)
                for cc in range(NT):
                    act.wait_ge(s_seg, g * 5 + cc + 2)
                    act.wait_ge(s_yd, g * 5 + cc + 1)
                    nc.scalar.activation(EE.rearrange("p d h n -> p (d h n)"), psf[:, 0:2048], ACT.Exp).then_inc(s_E, 1)

            for n in range(4 * NT):
                j, t = n // NT, n % NT
                act.wait_ge(s_z, n + 1)
                if n >= 2:
                    act.wait_ge(s_yz, n - 1)
                if n == 0:
                    act.wait_ge(s_y, SG * 5 + 1)
                nc.scalar.activation(ZS[n % 2], ps[:, n % 4, :], ACT.Silu).then_inc(s_zs, 1)
                if n >= 1:
                    m = n - 1
                    act.wait_ge(s_yz, m + 1)
                    order(nc.scalar.activation(YQ[0], Y[:, m % NT, (m // NT) * 512:(m // NT + 1) * 512], ACT.Square,
                                               accum_out=ssy[:, m % NT, m // NT:m // NT + 1]))
                    nc.scalar.activation(mk2[:, :], ssy[:, 0, 0:1], ACT.Copy).then_inc(s_yq, 1)
            m = 4 * NT - 1
            act.wait_ge(s_yz, m + 1)
            order(nc.scalar.activation(YQ[0], Y[:, m % NT, (m // NT) * 512:(m // NT + 1) * 512], ACT.Square,
                                       accum_out=ssy[:, m % NT, m // NT:m // NT + 1]))
            nc.scalar.activation(mk2[:, :], ssy[:, 0, 0:1], ACT.Copy).then_inc(s_yq, 1)
            act.wait_ge(s_ryv, 1)
            nc.scalar.activation(ry[:, :], ry[:, :], ACT.Sqrt).then_inc(s_ryd, 1)
            for n in range(2 * NT):
                t, b = n // 2, n % 2
                act.wait_ge(s_yt, n + 1)
                nc.scalar.activation(YT[b][:, :, t * P:(t + 1) * P],
                                     psf[:, b * 1024:b * 1024 + 1024].rearrange("p (k n) -> p k n", k=KD), ACT.Copy)\
                    .then_inc(s_yte, 1)
            moe(1)

        @block.vector
        def _(dve):
            for s in LED["dve"]:
                dve.sem_inc(s, 1)
            order = Order(dve, o_dve)

            def norm_rows(nn):
                half = nn % 2
                dve.wait_ge(s_mb[nn], 32)
                for cc in range(2):
                    order(nc.vector.scalar_tensor_tensor(MB[half][:, 1, cc, :], MB[half][:, 1, cc, :], 1.0, G,
                                                         op0=ALU.add, op1=ALU.mult))
                dve.wait_ge(s_ss, nn + 1)
                nc.vector.tensor_scalar(ssq[:, 0:NT], ssq[:, 0:NT], 1.0 / D, EPS, ALU.mult, ALU.add).then_inc(s_var, 1)
                dve.wait_ge(s_sd, nn + 1)
                order(nc.vector.reciprocal(ssq[:, 0:NT], ssq[:, 0:NT]))
                for t in range(NT):
                    nc.vector.scalar_tensor_tensor(H[:, t, :], X[:, t, :], ssq[:, t:t + 1],
                                                   MB[half][:, 1, min(t, 1), :],
                                                   op0=ALU.mult, op1=ALU.mult).then_inc(s_hm, 1)

            dve.wait_ge(s_init, 80)
            for l in range(2):
                wv = MR[:, l, :].rearrange("p (i j n) -> p j i n", j=3, n=512)
                with dve.Fori(0, 4) as i:
                    for j in range(3):
                        dve.wait_ge(s_wused[j], i + (4 * l + 1) + 1)
                        nc.vector.tensor_tensor(wv[:, j, i], ps[0:2, j, :], wv[:, j, i], ALU.add)\
                            .then_inc(s_modfree[j], 1)
            dve.wait_ge(s_x, 32)
            norm_rows(0)

            dve.wait_ge(s_gqk, 32)
            for t in range(NT):
                b = 3 * (t % 2) * 512
                dve.wait_ge(s_sq, t + 1)
                order(nc.vector.tensor_reduce(rs[:, :], SQ.rearrange("p (h d) -> p h d", d=HD), AX.X, ALU.add))
                nc.vector.tensor_scalar(rs[:, :], rs[:, :], 1.0 / HD, EPS, ALU.mult, ALU.add).then_inc(s_varq, 1)
                dve.wait_ge(s_sdq, t + 1)
                order(nc.vector.reciprocal(rs[:, :], rs[:, :]))
                order(nc.vector.tensor_scalar(rs[:, 0:NH], rs[:, 0:NH], HD ** -0.5, None, ALU.mult))
                if t == 1:
                    dve.wait_ge(s_qf, 1)
                nc.vector.tensor_tensor(QN.rearrange("p (h d) -> p h d", d=HD),
                                        psf[:, b:b + QK].rearrange("p (h d) -> p h d", d=HD),
                                        rs[:, :].unsqueeze(2).to_broadcast([P, NH + NKV, HD]), ALU.mult).then_inc(s_qn, 1)
                dve.wait_ge(s_qg, t + 1)
                if t >= 1:
                    dve.wait_ge(s_t2, t)
                    cos = tab[:, T_COS + (t - 1) * HD:T_COS + t * HD].unsqueeze(1).to_broadcast([P, NH + NKV, HD])
                    order(nc.vector.tensor_tensor(QN.rearrange("p (h d) -> p h d", d=HD),
                                                  QN.rearrange("p (h d) -> p h d", d=HD), cos, ALU.mult))
                    dve.wait_ge(s_tq, 3 * t)
                    nc.vector.tensor_tensor(QF, QN[:, 0:D], T2[:, 0:D], ALU.add)
                    nc.vector.tensor_tensor(KDUP,
                                            QN[:, D:QK].rearrange("p (g d) -> p g d", d=HD).unsqueeze(2).to_broadcast([P, NKV, 2, HD]),
                                            T2[:, D:QK].rearrange("p (g d) -> p g d", d=HD).unsqueeze(2).to_broadcast([P, NKV, 2, HD]),
                                            ALU.add).then_inc(s_qf, 1)
                else:
                    nc.vector.tensor_copy(QF, QN[:, 0:D])
                    nc.vector.tensor_copy(KOUT, QN[:, D:QK])
                    nc.vector.tensor_copy(KDUP, QN[:, D:QK].rearrange("p (g d) -> p g d", d=HD)
                                          .unsqueeze(2).to_broadcast([P, NKV, 2, HD])).then_inc(s_qf, 1)

            def softmax_parts(T, nk):
                def row_max(h):
                    dve.wait_ge(s_S, T * NH + h + 1)
                    nc.vector.tensor_reduce(nmx[:, h:h + 1], psf[:, 1024 * (h % 2):1024 * (h % 2) + nk * P],
                                            AX.X, ALU.max, negate=True).then_inc(s_max, 1)

                def turned(h):
                    u = T * NH + h
                    dve.wait_ge(s_T, u + 1)
                    if not (isinstance(T, int) and T == 0 and h < 2):
                        dve.wait_ge(s_pv, u - 1)
                    nc.vector.tensor_copy(PT[h % 2][:, 0:nk * P], psf[:, 2048:2048 + nk * P]).then_inc(s_pte, 1)

                def normed(half):
                    dve.wait_ge(s_pv, T * NH + 8 * half + 8)
                    hs = slice(8 * half, 8 * half + 8)
                    nc.vector.reciprocal(rden[:, hs], den[:, hs]).then_inc(o_rden, 1)
                    dve.wait_ge(o_rden, 2 * T + half + 1)
                    nc.vector.tensor_tensor(
                        OA[:, T, 512 * half:512 * half + 512].rearrange("p (h d) -> p h d", d=HD),
                        ps[:, 6 + half, :].rearrange("p (h d) -> p h d", d=HD),
                        rden[:, hs].unsqueeze(2).to_broadcast([P, 8, HD]), ALU.mult).then_inc(s_oev, 1)

                for s in range(NH + 1):
                    if s < NH:
                        row_max(s)
                    if s >= 1:
                        turned(s - 1)
                    if s == 10:
                        normed(0)
                normed(1)

            softmax_parts(0, 1)
            with dve.Fori(0, NT - 1) as i:
                softmax_parts(i + 1, 5)

            for t in range(NT):
                dve.wait_ge(s_op, t + 1)
                b = 2048 + 1024 * (t % 2)
                if t >= 1:
                    dve.wait_ge(s_x1, t)
                nc.vector.tensor_tensor(JUNK, psf[:, b:b + D], MB[0][:, 2, min(t, 1), :], ALU.mult).then_inc(s_opm, 1)

            def moe(l):
                nn = 2 * l + 1
                norm_rows(nn)
                V_ = nc.vector
                dve.wait_ge(ES["score"], l + 1)
                dve.wait_ge(s_rw, 32)
                order(V_.tensor_tensor(biased, score, RB[:, :].unsqueeze(1).to_broadcast([P, NT, NE]), ALU.add))
                bv = biased.rearrange("p t (g e) -> p (t g) e", g=NG)
                other = bv.unsqueeze(2).to_broadcast([P, NT * NG, EG, EG])
                own = bv.unsqueeze(3).to_broadcast([P, NT * NG, EG, EG])
                tie = tab[:, T_TIE:T_END].rearrange("p (e f) -> p e f", e=EG).unsqueeze(1)
                V_.tensor_tensor(above, other, own, ALU.is_gt)
                order(V_.tensor_tensor(equal, other, own, ALU.is_equal))
                order(V_.tensor_tensor(equal, equal, tie.to_broadcast([P, NT * NG, EG, EG]), ALU.mult))
                order(V_.tensor_tensor(above, above, equal, ALU.add))
                cv = chosen.rearrange("p t (g e) -> p (t g) e", g=NG)
                order(V_.tensor_reduce(cv, above, AX.X, ALU.add))
                order(V_.tensor_scalar(chosen, chosen, 1.5, None, ALU.is_lt))
                order(V_.tensor_tensor(weighted, chosen, biased, ALU.mult))
                order(V_.tensor_reduce(gsum.rearrange("p t g -> p (t g)"), weighted.rearrange("p t (g e) -> p (t g) e", g=NG),
                                       AX.X, ALU.add))
                ga, ge = above[:, 0:NT], equal[:, 0:NT]
                other = gsum.unsqueeze(2).to_broadcast([P, NT, NG, NG])
                own = gsum.unsqueeze(3).to_broadcast([P, NT, NG, NG])
                V_.tensor_tensor(ga, other, own, ALU.is_gt)
                order(V_.tensor_tensor(ge, other, own, ALU.is_equal))
                order(V_.tensor_tensor(ge, ge, tie.to_broadcast([P, NT, NG, NG]), ALU.mult))
                order(V_.tensor_tensor(ga, ga, ge, ALU.add))
                order(V_.tensor_reduce(gtop, ga, AX.X, ALU.add))
                order(V_.tensor_scalar(gtop, gtop, 0.5, None, ALU.is_lt))
                gt = gtop.rearrange("p t g -> p (t g)").unsqueeze(2).to_broadcast([P, NT * NG, EG])
                V_.tensor_tensor(cv, cv, gt, ALU.mult).then_inc(ES["sel"], 1)
                dve.wait_ge(ES["sel"], l + 1)
                order(V_.tensor_tensor(weighted, chosen, score, ALU.mult))
                order(V_.tensor_reduce(wsum, weighted, AX.X, ALU.add))
                order(V_.reciprocal(wsum, wsum))
                order(V_.tensor_tensor(weighted, weighted, wsum.unsqueeze(2).to_broadcast([P, NT, NE]), ALU.mult))
                order(V_.tensor_scalar(steps, tab[:, T_IOTA:T_IOTA + MAXT], float(P), None, ALU.mult))
                dve.wait_ge(ES["pos"], l + 1)
                V_.tensor_copy(place, ps[:, 5, 0:NT * NE].rearrange("p (t e) -> p t e", t=NT))
                order(V_.tensor_copy(count, ps[:, 5, NT * NE:(NT + 1) * NE]))
                order(V_.tensor_tensor(full, count.unsqueeze(2).to_broadcast([P, NE, NT]),
                                       steps[:, 0:NT].unsqueeze(1).to_broadcast([P, NE, NT]), ALU.is_gt))
                order(V_.tensor_reduce(tiles_of, full, AX.X, ALU.add))
                order(V_.tensor_tensor_scan(upto, tab[:, T_ONE:T_ONE + NE], tiles_of, 0.0, ALU.mult, ALU.add))
                order(V_.tensor_scalar(steps[0:1, :], tab[0:1, T_IOTA:T_IOTA + MAXT], 2.0, None, ALU.mult))
                order(V_.tensor_scalar(steps[0:1, :], steps[0:1, :], upto[0:1, NE - 1:NE], None, ALU.is_lt))
                order(V_.tensor_reduce(npf[:, :], steps[0:1, :], AX.X, ALU.add))
                V_.tensor_copy(npi[:, l:l + 1], npf[:, :])
                order(V_.tensor_tensor(ended[0:1], upto[0:1].unsqueeze(1).to_broadcast([1, MAXT, NE]),
                                       tab[0:1, T_IOTA:T_IOTA + MAXT].unsqueeze(2).to_broadcast([1, MAXT, NE]), ALU.is_le))
                order(V_.tensor_reduce(eotf[:, :], ended[0:1], AX.X, ALU.add))
                order(V_.tensor_scalar(eotf[:, :], eotf[:, :], NE - 1.0, None, ALU.min))
                V_.tensor_copy(eoti[:, :], eotf[:, :]).then_inc(ES["np"], 1)
                order(V_.tensor_tensor(base, upto, tiles_of, ALU.subtract))
                order(V_.tensor_scalar(base, base, float(P), 1.0, ALU.mult, ALU.add))
                order(V_.tensor_tensor(spot, place, base.unsqueeze(1).to_broadcast([P, NT, NE]), ALU.add))
                order(V_.tensor_tensor(spot, spot, chosen, ALU.mult))
                order(V_.tensor_reduce(slotf[:, 0, :], spot, AX.X, ALU.max))
                order(V_.tensor_reduce(tot, spot, AX.X, ALU.add))
                order(V_.tensor_tensor(slotf[:, 1, :], tot, slotf[:, 0, :], ALU.subtract))
                for a in range(2):
                    order(V_.tensor_tensor(mine, spot, slotf[:, a, :].unsqueeze(2).to_broadcast([P, NT, NE]), ALU.is_equal))
                    order(V_.tensor_tensor(mine, mine, weighted, ALU.mult))
                    order(V_.tensor_reduce(gate2[:, a, :], mine, AX.X, ALU.add))
                order(V_.tensor_scalar(slotf[:, :, :], slotf[:, :, :], 1.0, None, ALU.subtract))
                V_.tensor_copy(sloti[:, :, :], slotf[:, :, :]).then_inc(ES["slot"], 1)

                dve.wait_ge(ES["np"], l + 1)
                done = 0 if l == 0 else dve.value_load(npi[0:1, 0:1], min_val=1, max_val=MAXT // 2)
                pairs = dve.value_load(npi[0:1, l:l + 1], min_val=1, max_val=MAXT // 2)
                with dve.Fori(0, pairs) as i:
                    turn = i + done
                    for j in range(2):
                        dve.wait_ge(ES["silu"], turn * 2 + j + 1)
                        dve.wait_ge(ES["at"], turn * 2 + 1)
                        V_.tensor_tensor(AC[j], ps[:, 4 + j, FF:2 * FF], SG_[j], ALU.mult).then_inc(ES["act"], 1)
                for t in range(NT):
                    a, b = GY[t % 2]
                    dve.wait_ge(ES["wa"], l * NT + t + 1)
                    order(V_.scalar_tensor_tensor(b, b, gate2[:, 1, t:t + 1], a, op0=ALU.mult, op1=ALU.add))
                    V_.tensor_tensor(b, b, MB[1][:, 2, min(t, 1), :], ALU.mult).then_inc(ES["wg"], 1)

            moe(0)
            norm_rows(2)
            V_ = nc.vector
            dve.wait_ge(s_pre_pe, 2)
            dve.wait_ge(s_ssdin, 96)
            dve.wait_ge(s_pre_act, 1)
            bias = DTB.rearrange("p (d h) -> p d h", d=2).unsqueeze(1).to_broadcast([P, NT, 2, SH])
            order(V_.tensor_tensor(sp0, ps[:, 6, 0:320].rearrange("p (t d h) -> p t d h", t=NT, d=2), bias, ALU.add))
            order(V_.tensor_scalar(sp1, sp0, -1.0, None, ALU.mult))
            V_.tensor_tensor(sp1, sp1, sp0, ALU.min).then_inc(s_pre_dve, 1)
            dve.wait_ge(s_pre_act, 2)
            V_.tensor_scalar(sp2, sp1, 1.0, None, ALU.add).then_inc(s_pre_dve, 1)
            dve.wait_ge(s_pre_dve, 2)
            dve.wait_ge(s_pre_act, 4)
            order(V_.tensor_scalar(sp2, sp2, 1.0, None, ALU.subtract))
            order(V_.tensor_scalar(sp4, sp2, 0.0, None, ALU.is_equal))
            V_.tensor_tensor(sp3, sp3, sp4, ALU.add)
            order(V_.tensor_tensor(sp2, sp2, sp4, ALU.add))
            order(V_.reciprocal(sp2, sp2))
            order(V_.tensor_tensor(sp3, sp3, sp1, ALU.mult))
            order(V_.tensor_tensor(sp3, sp3, sp2, ALU.mult))
            order(V_.tensor_scalar(sp0, sp0, 0.0, None, ALU.max))
            order(V_.tensor_tensor(DTA, sp0, sp3, ALU.add))
            dve.wait_ge(s_pre_act, 3)
            am = AROW.rearrange("p (d h) -> p d h", d=2).unsqueeze(1).to_broadcast([P, NT, 2, SH])
            order(V_.tensor_tensor(DA, DTA, am, ALU.mult))
            V_.tensor_scalar(DA, DA, -1.0, None, ALU.mult).then_inc(s_pre_dve, 1)
            dve.wait_ge(s_pre_act, 7)
            V_.tensor_tensor(DTD, DTA, sp0, ALU.mult).then_inc(s_pre_dve, 1)
            dve.wait_ge(s_pre_dve, 4)

            dve.wait_ge(s_ssdin, 96)
            with dve.Fori(0, SG) as g:
                heads = bass.ds(g * HG, HG)
                for st in range(6):
                    ch = (g * 4 + st) if st < 4 else (g + 16 + 4 * (st - 4))
                    dve.wait_ge(s_c0, g * 6 + st + 1)
                    for i, j in enumerate((0, 1, 3, 4)):
                        x = V_.scalar_tensor_tensor(AC2[st % 2], U[st % 2][:, j:j + AW],
                                                    CW[:, bass.ds(ch, 1), j:j + 1].rearrange("p a b -> p (a b)"), AC2[st % 2],
                                                    op0=ALU.mult, op1=ALU.add)
                        if i < 3:
                            x.then_inc(o_cv, 1)
                            dve.wait_ge(o_cv, g * 18 + 3 * st + i + 1)
                    x.then_inc(s_cv, 1)
                for i, (d, cc) in enumerate(UNITS[:6]):
                    src, dst = (cc - 1, cc) if d == 0 else (cc - 1, cc - 2)
                    if i < 2:
                        dve.wait_ge(s_rte, g * 2 + d + 1)
                    if i >= 2:
                        dve.wait_ge(s_ste, g * 6 + i - 1)
                    V_.tensor_tensor(PV[:, d, dst, :].rearrange("p (h n) -> p h n", h=HG),
                                     PV[:, d, src, :].rearrange("p (h n) -> p h n", h=HG),
                                     CD[:, cc, d, heads].unsqueeze(2).to_broadcast([P, HG, SP]), ALU.mult).then_inc(o_pv, 1)
                    dve.wait_ge(o_pv, g * 6 + i + 1)
                    dve.wait_ge(s_st, g * 8 + i + 1)
                    V_.tensor_tensor(PV[:, d, dst, :], PV[:, d, dst, :], ps[:, 4 + i % 2, :], ALU.add).then_inc(s_ste, 1)

                def x_times_dt(cc):
                    dve.wait_ge(s_yd, g * 5 + cc + 1)
                    for d in range(2):
                        x = V_.tensor_tensor(XS[:, d], XT[:, cc, :].rearrange("p (h n) -> p h n", h=HG),
                                             DTA[:, cc, d, heads].unsqueeze(2).to_broadcast([P, HG, SP]), ALU.mult)
                    x.then_inc(s_xs, 1)

                def cb_masked(cc):
                    dve.wait_ge(s_cb, g * 5 + cc + 1)
                    dve.wait_ge(s_M, g * 5 + cc + 1)
                    for d in range(2):
                        x = V_.tensor_tensor(CB[:, d, :], ps[:, 5, 0:P], tab[:, MASK[d]:MASK[d] + P], ALU.mult)
                    x.then_inc(s_cbm, 1)

                def weights(cc):
                    dve.wait_ge(s_cbm, g * 5 + cc + 2)
                    dve.wait_ge(s_E, g * 5 + cc + 2)
                    for d in range(2):
                        x = V_.tensor_tensor(EE[:, d], EE[:, d], CB[:, d, :].unsqueeze(1).to_broadcast([P, HG, P]), ALU.mult)
                    x.then_inc(s_M, 1)

                def add_up(cc):
                    y = Y[:, cc, bass.ds(g * 512, 512)]
                    yh = y.rearrange("p (h n) -> p h n", h=HG)
                    th = TMP.rearrange("p (h n) -> p h n", h=HG)
                    dve.wait_ge(s_D, g * 5 + cc + 2)
                    dve.wait_ge(s_yd, g * 5 + cc + 2)
                    k = 0
                    if cc >= 1:
                        dve.wait_ge(s_yo, g * 4 + cc)
                        for d in range(2):
                            V_.tensor_tensor(th, ps[:, 6 + d, :].rearrange("p (h n) -> p h n", h=HG),
                                             EA[:, cc, d, heads].unsqueeze(2).to_broadcast([P, HG, SP]), ALU.mult).then_inc(o_y, 1)
                            dve.wait_ge(o_y, g * 16 + 4 * (cc - 1) + 2 * d + 1)
                            V_.tensor_tensor(y, y, TMP, ALU.add).then_inc(o_y, 1)
                            dve.wait_ge(o_y, g * 16 + 4 * (cc - 1) + 2 * d + 2)
                    V_.tensor_tensor(y, y, ps[:, 4, :], ALU.add).then_inc(s_y, 1)

                for cc in range(NT):
                    cb_masked(cc)
                    x_times_dt(cc)
                    if cc >= 1:
                        add_up(cc - 1)
                    weights(cc)
                add_up(NT - 1)

            for n in range(4 * NT):
                j, t = n // NT, n % NT
                y = Y[:, t, j * 512:(j + 1) * 512]
                dve.wait_ge(s_zs, n + 1)
                if n == 0:
                    dve.wait_ge(s_y, SG * 5 + 1)
                V_.tensor_tensor(y, y, ZS[n % 2], ALU.mult).then_inc(s_yz, 1)
            dve.wait_ge(s_yq, 4 * NT)
            order(V_.tensor_reduce(ry[:, :], ssy[:, :, :], AX.X, ALU.add))
            V_.tensor_scalar(ry[:, :], ry[:, :], 1.0 / DI, EPS, ALU.mult, ALU.add).then_inc(s_ryv, 1)
            dve.wait_ge(s_ryd, 1)
            order(V_.reciprocal(ry[:, :], ry[:, :]))
            dve.wait_ge(s_yg, 4 * NT)
            for n in range(2 * NT):
                a, t = n // NT, n % NT
                dve.wait_ge(s_op2, n + 1)
                if n >= 2:
                    dve.wait_ge(s_xadd, n - 1) if n - 1 <= NT else dve.wait_ge(s_x1, n - 1)
                V_.scalar_tensor_tensor(OM[n % 2], ps[:, 4 + n % 4, :], ry[:, t:t + 1], MB[0][:, 2, min(t, 1), a * 512:(a + 1) * 512],
                                        op0=ALU.mult, op1=ALU.mult).then_inc(s_om, 1)
            moe(1)

        @block.gpsimd
        def _(pool):
            for s in LED["pool"]:
                pool.sem_inc(s, 1)
            def norm_shift(nn):
                for t in range(NT):
                    pool.wait_ge(s_hm, nn * NT + t + 1)
                    nc.gpsimd.tensor_tensor(H[:, t, :], H[:, t, :], MB[nn % 2][:, 0, min(t, 1), :], ALU.add)\
                        .then_inc(s_h, 1)

            def spread_modulation(l, half):
                pool.wait_ge(s_modst[2 * l + half], 16)
                pool.dma_start(MB[half].rearrange("p f c n -> p (f c n)"),
                               mod_d[l, half].rearrange("f c n -> (f c n)").partition_broadcast(P))\
                    .then_inc(s_mb[2 * l + half], 16)

            for l in range(2):
                for half in range(2):
                    for j in range(3):
                        pool.wait_ge(s_modfree[j], 4 * l + 2 * half + 2 + 1)
                    pool.dma_start(mod_d[l, half].rearrange("f c n -> c f n"),
                                   MR[:, l, half * 3 * D:(half + 1) * 3 * D].rearrange("c (f n) -> c f n", f=3)).then_inc(s_modst[2 * l + half], 16)
                    if l == 0 and half == 0:
                        spread_modulation(0, 0)
            for i in range(4):
                pool.wait_ge(s_modst[i], 16)
            nc.gpsimd.memset(mark[:, :], 0.0)
            nc.gpsimd.memset(zeros, 0.0).then_inc(s_zero, 1)
            pool.dma_start(G, norm1_g[0].partition_broadcast(P)).then_inc(s_mb[0], 16)
            norm_shift(0)

            pool.wait_ge(s_ht, NT)
            pool.dma_start(KDC[:, :, 0, :], cache_k[0, 0]).then_inc(s_kv, 16)
            pool.dma_start(KDC[:, :, 1, :], cache_k[0, 0]).then_inc(s_kv, 16)
            pool.dma_start(V[:, NT, :], cache_v[0, 0].rearrange("p g d -> p (g d)")).then_inc(s_kv, 16)
            pool.wait_ge(s_gqk, 32)
            for t in range(NT):
                pool.wait_ge(s_qn, t + 1)
                nc.gpsimd.tensor_tensor(QN[:, 0:D].rearrange("p (h d) -> p h d", d=HD),
                                        QN[:, 0:D].rearrange("p (h d) -> p h d", d=HD),
                                        gqk[:, 0, :].unsqueeze(1).to_broadcast([P, NH, HD]), ALU.mult)
                nc.gpsimd.tensor_tensor(QN[:, D:QK].rearrange("p (h d) -> p h d", d=HD),
                                        QN[:, D:QK].rearrange("p (h d) -> p h d", d=HD),
                                        gqk[:, 1, :].unsqueeze(1).to_broadcast([P, NKV, HD]), ALU.mult).then_inc(s_qg, 1)
                if t >= 1:
                    pool.wait_ge(s_qg, t + 1)
                    sin = tab[:, T_SIN + (t - 1) * HD:T_SIN + t * HD].rearrange("p (a d) -> p a d", a=2)
                    qv = QN.rearrange("p (h a d) -> p a h d", a=2, d=HD // 2)
                    tv = T2.rearrange("p (h a d) -> p a h d", a=2, d=HD // 2)
                    if t >= 2:
                        pool.wait_ge(s_qf, t)
                    for a in range(2):
                        last = nc.gpsimd.tensor_tensor(tv[:, a], qv[:, 1 - a],
                                                       sin[:, a, :].unsqueeze(1).to_broadcast([P, NH + NKV, HD // 2]), ALU.mult)
                    last.then_inc(s_t2, 1)
            pool.wait_ge(s_qf, 1)
            pool.dma_start(new_k[0, 0].rearrange("p g d -> p (g d)"), KOUT).then_inc(s_out, 16)
            pool.dma_start(new_v[0, 0].rearrange("p g d -> p (g d)"), V[:, 0, :]).then_inc(s_out, 16)

            def query_columns(T):
                nc.gpsimd.tensor_copy(QC, QT[:, :, bass.ds(T * P, P)] if not isinstance(T, int)
                                      else QT[:, :, T * P:(T + 1) * P]).then_inc(s_qc, 1)

            pool.wait_ge(s_tqe, 16)
            query_columns(0)
            with pool.Fori(0, NT - 1) as i:
                pool.wait_ge(s_S, (i + 1) * NH)
                query_columns(i + 1)
            for t in range(NT):
                pool.wait_ge(s_opm, t + 1)
                nc.gpsimd.tensor_tensor(X[:, t, :], X[:, t, :], JUNK, ALU.add).then_inc(s_x1, 1)
            def moe(l):
                nn = 2 * l + 1
                norm_shift(nn)
                pool.wait_ge(ES["slot"], l + 1)
                if l == 0:
                    pool.wait_ge(s_clear, 16)
                for t in range(NT):
                    pool.wait_ge(s_h, nn * NT + t + 1)
                    for a in range(2):
                        pool.indirect_dma_start(xs_d, bass.IndirectOffsetOnAxis(ap=sloti[:, a, t:t + 1], axis=0),
                                                H[:, t, :], None).then_inc(ES["sc"], 16)
                done = 0 if l == 0 else pool.value_load(npi[0:1, 0:1], min_val=1, max_val=MAXT // 2)
                pairs = pool.value_load(npi[0:1, l:l + 1], min_val=1, max_val=MAXT // 2)
                for j in range(2):
                    pool.wait_ge(ES["yst"][j], (pairs + done) * 16 + 1)
                nc.gpsimd.tensor_tensor(mark[:, :], mark[:, :], mark[:, :], ALU.add).then_inc(ES["all"], 1)
                pool.wait_ge(ES["all"], l + 1)
                pool.wait_ge(ES["sc"], 2 * NT * 16 * (l + 1))
                for t in range(NT + 2):
                    if t >= 2:
                        pool.wait_ge(ES["wg"], l * NT + t - 1)
                        nc.gpsimd.tensor_tensor(X[:, t - 2, :], X[:, t - 2, :], GY[t % 2][1], ALU.add).then_inc(ES["x2"], 1)
                        if l == 1:
                            pool.wait_ge(ES["x2"], l * NT + t - 1)
                            pool.dma_start(y_prompt[0] if t == 2 else y_sample[0, (t - 3) * P:(t - 2) * P, :], X[:, t - 2, :])\
                                .then_inc(s_out, 16)
                    if t < NT:
                        if t >= 2:
                            pool.wait_ge(ES["x2"], l * NT + t - 1)
                        for a in range(2):
                            pool.indirect_dma_start(GY[t % 2][a], None, xs_d,
                                                    bass.IndirectOffsetOnAxis(ap=sloti[:, a, t:t + 1], axis=0))\
                                .then_inc(ES["gat"][t % 2], 16)

            pool.wait_ge(s_ot, NT)
            spread_modulation(0, 1)
            pool.wait_ge(s_ht, 5)
            pool.dma_start(G, norm2_g[0].partition_broadcast(P)).then_inc(s_mb[1], 16)
            moe(0)
            pool.wait_ge(s_opm, NT)
            spread_modulation(1, 0)
            pool.wait_ge(s_hm, 2 * NT)
            pool.dma_start(G, norm1_g[1].partition_broadcast(P)).then_inc(s_mb[2], 16)
            norm_shift(2)
            P_ = nc.gpsimd
            pool.wait_ge(s_hm, 3 * NT)
            pool.wait_ge(s_h, 3 * NT)
            for i in range(2):
                last = P_.memset(U[i], 0.0)
            last.then_inc(s_pad, 1)
            pool.wait_ge(s_pad, 1)
            pool.wait_ge(s_pre_dve, 4)
            pool.wait_ge(s_ssdin, 96)
            pool.wait_ge(s_ht, 3 * NT)
            with pool.Fori(0, SG) as g:
                heads = bass.ds(g * HG, HG)

                def da_masked(cc):
                    pool.wait_ge(s_seg, g * 5 + cc + 1)
                    for d in range(2):
                        x = P_.tensor_tensor(RR[:, d], DA[:, cc, d, heads].unsqueeze(2).to_broadcast([P, HG, P]),
                                             tab[:, MASK[d]:MASK[d] + P].unsqueeze(1).to_broadcast([P, HG, P]), ALU.mult)
                    x.then_inc(s_R, 1)

                da_masked(0)
                pool.wait_ge(s_txe, g * 5 + 4)
                for i, (d, cc) in enumerate(UNITS):
                    if i >= 2:
                        pool.wait_ge(s_st, g * 8 + i - 1)
                    P_.tensor_tensor(XD[:, d], XT[:, cc, :].rearrange("p (h n) -> p h n", h=HG),
                                     DTD[:, cc, d, heads].unsqueeze(2).to_broadcast([P, HG, SP]), ALU.mult).then_inc(s_xsd, 1)
                for cc in range(NT):
                    P_.tensor_tensor(Y[:, cc, bass.ds(g * 512, 512)].rearrange("p (h n) -> p h n", h=HG),
                                     XT[:, cc, :].rearrange("p (h n) -> p h n", h=HG),
                                     DROW[:, heads].unsqueeze(2).to_broadcast([P, HG, SP]), ALU.mult).then_inc(s_D, 1)
                    if cc >= 1:
                        da_masked(cc)
            pool.wait_ge(s_ngr, 16)
            for n in range(4 * NT):
                j, t = n // NT, n % NT
                y = Y[:, t, j * 512:(j + 1) * 512]
                pool.wait_ge(s_yq, n + 1)
                P_.tensor_tensor(y, y, NGR[:, j * 512:(j + 1) * 512], ALU.mult).then_inc(s_yg, 1)
            pool.wait_ge(s_yg, 4 * NT)
            spread_modulation(1, 1)
            for n in range(2 * NT):
                a, t = n // NT, n % NT
                x = X[:, t, a * 512:(a + 1) * 512]
                pool.wait_ge(s_om, n + 1)
                P_.tensor_tensor(x, x, OM[n % 2], ALU.add).then_inc(s_xadd if a == 0 else s_x1, 1)
            pool.wait_ge(s_yt, 2 * NT)
            pool.dma_start(G, norm2_g[1].partition_broadcast(P)).then_inc(s_mb[3], 16)
            moe(1)
            pool.wait_ge(s_fso[0], SG * 16 + 1)
            pool.wait_ge(s_fso[1], SG * 16 + 1)
            pool.wait_ge(s_out, 16 * (NT + 2))


_INS = ["x_prompt", "x_sample", "c", "c_ctx", "cache_k", "cache_v", "state_ssm", "mod_w", "mod_b", "norm1_g",
        "norm2_g", "attn_w_qkv", "attn_q_norm_g", "attn_k_norm_g", "attn_w_o", "ssd_in_proj", "ssd_conv_w",
        "ssd_conv_b", "ssd_dt_bias", "ssd_a_log", "ssd_d", "ssd_norm_g", "ssd_out_proj", "router_w", "router_b",
        "expert_w_gate", "expert_w_up", "expert_w_down"]
_OUTS = [(1, SEQ, D), (1, DEC, D), (1, 1, SEQ, NKV, HD), (1, 1, SEQ, NKV, HD), (1, 1, 2, SH, SP, SN)]


def kernel(**inputs):
    import concourse.bacc as bacc
    from concourse.bass_utils import run_bass_kernel_spmd as run

    nc = bacc.Bacc("TRN2", target_bir_lowering=False, num_devices=1)
    arrays, args = {}, []
    for name, a in [(n, inputs[n]) for n in _INS] + [("tables", tables())]:
        a = np.ascontiguousarray(a)
        arrays[f"in_{name}"] = a
        args.append(nc.dram_tensor(f"in_{name}", a.shape, mybir.dt.from_np(a.dtype), kind="ExternalInput").ap())
    for i, shape in enumerate(_OUTS):
        args.append(nc.dram_tensor(f"out_{i}", shape, F32, kind="ExternalOutput").ap())
    backbone(nc, *args)
    r = run(nc, [arrays], core_ids=[0])
    return tuple(r.results[0][f"out_{i}"] for i in range(len(_OUTS)))
```

```python
import math
import numpy as np
import concourse.bass as bass
from concourse import mybir
from contextlib import ExitStack

F32 = mybir.dt.float32
I32 = mybir.dt.int32
U32 = mybir.dt.uint32
ALU = mybir.AluOpType
ACT = mybir.ActivationFunctionType
AX = mybir.AxisListType

P = 128
D = 1024
KD = D // P
SEQ, DEC = 128, 512
TOK = SEQ + DEC
NT = TOK // P
PAST = 128
GRID_W = 64
NH, NKV, HD = 16, 4, 64
QK = (NH + NKV) * HD
DI = 2048
SH, SG, SP, SN = 32, 4, 64, 128
HG = SH // SG
NE, NG, EG = 16, 4, 4
FF = D // 4
EPS = 1e-6
MAXT = (2 * TOK - NE) // P + NE + 1
MAXT += MAXT % 2
PG = 1024

T_ID, T_UP, T_LOW, T_GT, T_LT, T_ONE = (i * P for i in range(6))
T_COS = 6 * P
T_SIN = T_COS + (NT - 1) * HD
T_IOTA = T_SIN + (NT - 1) * HD
T_TIE = T_IOTA + MAXT
T_END = T_TIE + NE


def tables():
    t = np.zeros((P, T_END), np.float32)
    r, c = np.arange(P)[:, None], np.arange(P)[None, :]
    for at, m in ((T_ID, r == c), (T_UP, r <= c), (T_LOW, r >= c), (T_GT, r > c), (T_LT, r < c), (T_ONE, r >= 0)):
        t[:, at:at + P] = m
    n_freq = HD // 4
    inv = (1.0 / (np.float32(10000.0) ** (np.arange(n_freq, dtype=np.float32) / n_freq))).astype(np.float32)
    pos = np.arange(DEC)
    ang = np.concatenate([(pos // GRID_W)[:, None].astype(np.float32) * inv,
                          (pos % GRID_W)[:, None].astype(np.float32) * inv], axis=1)
    cs = np.cos(ang).reshape(NT - 1, P, 2 * n_freq).transpose(1, 0, 2)
    sn = np.sin(ang).reshape(NT - 1, P, 2 * n_freq).transpose(1, 0, 2)
    t[:, T_COS:T_SIN] = np.concatenate([cs, cs], axis=2).reshape(P, -1)
    t[:, T_SIN:T_IOTA] = np.concatenate([-sn, sn], axis=2).reshape(P, -1)
    t[:, T_IOTA:T_TIE] = np.arange(MAXT)[None, :]
    e = np.arange(EG)
    t[:, T_TIE:T_END] = (e[None, :] < e[:, None]).reshape(1, -1)
    return t


class Order:

    def __init__(self, eng, sem):
        self.eng, self.sem, self.n = eng, sem, 0

    def __call__(self, ins):
        ins.then_inc(self.sem, 1)
        self.n = self.n + 1
        self.eng.wait_ge(self.sem, self.n)


def backbone(nc, x_prompt, x_sample, c, c_ctx, cache_k, cache_v, state_ssm, mod_w, mod_b, norm1_g, norm2_g,
             w_qkv, q_g, k_g, w_o, in_proj, conv_w, conv_b, dt_bias, a_log, ssd_d, ssd_g, out_proj,
             router_w, router_b, w_gate, w_up, w_down, consts,
             y_prompt, y_sample, new_k, new_v, new_ssm):
    mod_d = nc.dram_tensor("mod_rows", (2, 2, 2, 3, D), F32, kind="Internal").ap()
    ctx = ExitStack()
    with ctx:
        def sb(name, shape, dt=F32):
            return ctx.enter_context(nc.sbuf_tensor(name, shape, dt))

        def sem(name):
            return ctx.enter_context(nc.semaphore(name))

        def sems(name, n):
            return [sem(f"{name}{i}") for i in range(n)]

        mem = sb("mem", [P, 50 * PG])
        tab = sb("tab", [P, T_END])
        ps = ctx.enter_context(nc.psum_tensor("ps", [P, 8, 512], F32))
        psf = ps[:, :, :].rearrange("p b n -> p (b n)")

        def page(at, n, parts=P):
            a = int(at * PG)
            return mem[0:parts, a:a + n]

        ident = tab[:, T_ID:T_ID + P]
        X = page(0, NT * D).rearrange("p (t n) -> p t n", t=NT)
        HT = page(5, KD * TOK).rearrange("p (k n) -> p k n", k=KD)
        WS = [page(10 + 4 * i, 4 * PG).rearrange("p (k n) -> p k n", k=KD) for i in range(3)]
        MB_ROWS = 3 * KD
        ROWS0 = page(33, P)
        COLS0 = page(33.125, P)
        bias_cols = COLS0[:, 2 * KD:2 * KD + 4 * MB_ROWS]
        g1_cols = COLS0[:, 2 * KD + 4 * MB_ROWS:].rearrange("p (l k) -> p l k", l=2)
        MODC = page(33.25, 8 * MB_ROWS).rearrange("p (c b) -> p c b", c=2)
        MS = page(38, 512, 2)
        MROW = page(33.5, 2 * P, 3 * MB_ROWS).rearrange("b (c n) -> b c n", c=2)
        MB = [page(22 + 6 * i, 6 * D).rearrange("p (f c n) -> p f c n", f=3, c=2) for i in range(2)]
        small = sb("small", [P, NT * 2 * SH])
        AB = small[:, 0:8 * KD].rearrange("p (l a c k) -> p l a c k", l=2, a=2, c=2)
        CUM = small[:, :].rearrange("p (t d h) -> p t d h", t=NT, d=2)
        condT = small[:, NT * 2 * SH - 2 * KD:].rearrange("p (c k) -> p c k", c=2)
        H = page(34, NT * D).rearrange("p (t n) -> p t n", t=NT)
        SQX = H[:, NT - 1, :]
        JUNK, G = page(39, D), page(40, D)
        ssq = sb("ssq", [P, 8])
        V = page(34, 6 * 256).rearrange("p (t n) -> p t n", t=6)
        QN = page(35.5, QK)
        SQ = page(36.75, QK)
        T2 = page(38, QK)
        QF = page(39.25, D)
        KDUP = page(40.25, 512).rearrange("p (g two d) -> p g two d", g=NKV, two=2)
        KDC = page(49, 512).rearrange("p (g two d) -> p g two d", g=NKV, two=2)
        KOUT = page(49.5, 256)
        QT = page(41, 8 * TOK).rearrange("p (m n) -> p m n", m=8)
        KT = page(46, 4 * 768).rearrange("p (g n) -> p g n", g=4)
        gqk = small[:, P:2 * P].rearrange("p (a d) -> p a d", a=2)
        rs = sb("rs", [P, NH + NKV])
        PR = [page(35.5 + 0.625 * i, 640) for i in range(2)]
        PT = [page(36.75 + 0.625 * i, 640) for i in range(2)]
        QC = page(39.25, D).rearrange("p (m n) -> p m n", m=8)
        OA = page(28, NT * D).rearrange("p (t n) -> p t n", t=NT)
        nmx = small[:, 2 * P:2 * P + NH]
        den = small[:, 2 * P + NH:2 * P + 2 * NH]
        rden = small[:, 2 * P + 2 * NH:2 * P + 3 * NH]

        RW = sb("RW", [P, KD, NE])
        RB = sb("RB", [P, NE])
        mark, mk2 = sb("mark", [P, 1]), sb("mk2", [P, 1])
        zeros = page(49.75, 256)
        route = page(41, 2048)

        def cut(at, *shape):
            v = route[:, at:at + math.prod(shape)]
            return v if len(shape) == 1 else v.rearrange("p (a b) -> p a b", a=shape[0]) if len(shape) == 2 \
                else v.rearrange("p (a b c) -> p a b c", a=shape[0], b=shape[1])

        score, biased, chosen, weighted = (cut(80 * i, NT, NE) for i in range(4))
        above, equal = cut(320, NT * NG, EG, EG), cut(640, NT * NG, EG, EG)
        place, spot, mine = (cut(960 + 80 * i, NT, NE) for i in range(3))
        gsum, gtop = cut(1200, NT, NG), cut(1220, NT, NG)
        count, tiles_of, upto, base = (cut(1240 + 16 * i, NE) for i in range(4))
        wsum, tot = cut(1304, NT), cut(1312, NT)
        steps = cut(1320, MAXT)
        full = cut(1360, NE, NT)
        ended = cut(1440, MAXT, NE)
        gate2 = sb("gate2", [P, 2, NT])
        slotf = sb("slotf", [P, 2, NT])
        sloti = sb("sloti", [P, 2, NT], U32)
        eotf, eoti = sb("eotf", [1, MAXT]), sb("eoti", [1, MAXT], I32)
        npf, npi = sb("npf", [1, 1]), sb("npi", [1, 2], I32)
        XG = [page(43 + i, D) for i in range(2)]
        XGT = [page(45 + i, D).rearrange("p (k n) -> p k n", k=KD) for i in range(2)]
        YO = [page(47 + i, D) for i in range(2)]
        SG_, AC, AT = ([page(39 + 0.75 * i + 0.25 * j, FF) for i in range(2)] for j in range(3))
        WD = [page(18 + 2 * i, 2 * D).rearrange("p (k n) -> p k n", k=2) for i in range(2)]
        GY = [[page(34 + 2 * i + j, D) for j in range(2)] for i in range(2)]
        cum_d = nc.dram_tensor("cum_rows", (NT * 2 * SH, P), F32, kind="Internal").ap()
        xs_d = nc.dram_tensor("slot_rows", (MAXT * P, D), F32, kind="Internal").ap()

        Y = page(34, NT * DI).rearrange("p (t n) -> p t n", t=NT)
        XT = page(44, NT * 512).rearrange("p (t n) -> p t n", t=NT)
        BT, CT = page(46.5, TOK), page(47.125, TOK)
        BK = page(47.75, NT * P).rearrange("p (t n) -> p t n", t=NT)
        CB = page(48.375, 2 * P).rearrange("p (d n) -> p d n", d=2)
        DTA, DA, EA, DTD = (page(48.625, 4 * 320)[:, 320 * i:320 * (i + 1)].rearrange("p (t d h) -> p t d h", t=NT, d=2)
                            for i in range(4))
        RR = page(28, 2048).rearrange("p (d h n) -> p d h n", d=2, h=HG)
        EE = page(30, 2048).rearrange("p (d h n) -> p d h n", d=2, h=HG)
        XS = page(32, 1024).rearrange("p (d h n) -> p d h n", d=2, h=HG)
        XD = page(33, 1024).rearrange("p (d h n) -> p d h n", d=2, h=HG)
        PV = page(18, 4096).rearrange("p (d c n) -> p d c n", d=2, c=NT - 1)
        UW = 2 + DEC + 2 + SEQ + 2
        AW = UW - 4
        U, AC2, CVT = ([page(22, 4096)[:, 650 * (2 * a + i):650 * (2 * a + i) + w] for i in range(2)]
                       for a, w in ((0, UW), (1, AW), (2, TOK)))
        RAW = page(16, 1024).rearrange("p (d a n) -> p d a n", d=2, a=4)
        NGT = page(49.9, 2 * KD)
        NGROWS = page(31, P, 2 * KD)
        CW = page(17.5, 144).rearrange("p (c j) -> p c j", j=6)
        DROW = page(17.5, 512)[:, 144:144 + SH]
        CD = page(17.5, 512)[:, 176:176 + 320].rearrange("p (t d h) -> p t d h", t=NT, d=2)
        WX = WS[0]
        WBC = page(14, 2048).rearrange("p (k n) -> p k n", k=KD)
        WDT = page(33, 512).rearrange("p (k n) -> p k n", k=KD)
        CWR = page(28, 3072, 6)
        DTB, AROW = page(32, 64), page(32, 128)[:, 64:128]
        sp0, sp1, sp2, sp3, sp4 = (page(28, 5 * 320)[:, 320 * i:320 * (i + 1)].rearrange("p (t d h) -> p t d h", t=NT, d=2)
                                   for i in range(5))
        CROWS = page(30.5, 3 * P)
        ZS = [page(33 + 0.5 * i, 512) for i in range(2)]
        ssy = sb("ssy", [P, NT, 4])
        ry = sb("ry", [P, NT])
        YT = [HT, page(44, KD * TOK).rearrange("p (k n) -> p k n", k=KD)]
        OM = [page(i, 512) for i in (42, 49)]
        WO = [[page(22, 4096).rearrange("p (k n) -> p k n", k=KD), WS[0]], [WS[2], WS[1]]]

        s_init, s_x = sem("s_init"), sem("s_x")
        s_condT, s_condS = sem("s_condT"), sem("s_condS")
        s_w = sems("s_w", 3)
        s_wused = sems("s_wused", 3)
        s_mc, s_mt, s_mrow = sem("s_mc"), sem("s_mt"), sem("s_mrow")
        s_ms, s_mturn, s_mcols = sem("s_ms"), sem("s_mturn"), sem("s_mcols")
        s_apd, s_apa = sem("s_apd"), sem("s_apa")
        s_modst = sems("s_modst", 2)
        s_mb = sems("s_mb", 4)
        o_dve, o_act, o_pool = sem("o_dve"), sem("o_act"), sem("o_pool")
        s_amod = sem("s_amod")
        s_ss, s_var, s_sd = sem("s_ss"), sem("s_var"), sem("s_sd")
        s_hm, s_h, s_ht, s_hT = sem("s_hm"), sem("s_h"), sem("s_ht"), sem("s_hT")
        s_gqk, s_kv = sem("s_gqk"), sem("s_kv")
        s_qkv, s_sq, s_v, s_varq, s_sdq, s_qn, s_qg, s_t2, s_qf, s_tq, s_tqe = (
            sem(n) for n in "s_qkv s_sq s_v s_varq s_sdq s_qn s_qg s_t2 s_qf s_tq s_tqe".split())
        s_S, s_max, s_exp, s_T, s_pte, s_pv, s_oev, s_qc = (
            sem(n) for n in "s_S s_max s_exp s_T s_pte s_pv s_oev s_qc".split())
        s_ot, s_otT, s_op, s_opm, s_x1 = (sem(n) for n in "s_ot s_otT s_op s_opm s_x1".split())
        o_rden = sem("o_rden")
        o_u, o_cv, o_pv, o_y = sem("o_u"), sem("o_cv"), sem("o_pv"), sem("o_y")

        s_rw, s_zero, s_clear = sem("s_rw"), sem("s_zero"), sem("s_clear")

        s_ssdin, s_pre_pe, s_pre_act, s_pre_dve = (sem(n) for n in "s_ssdin s_pre_pe s_pre_act s_pre_dve".split())
        (s_wx, s_wbc, s_raw, s_ip, s_u, s_c0, s_cv, s_sl, s_tx, s_txe, s_rt, s_rte, s_xsd, s_st, s_ste, s_fs, s_cb,
         s_cbm, s_E, s_M, s_xs, s_yd, s_yo, s_y, s_D, s_pad) = (sem(n) for n in (
            "s_wx s_wbc s_raw s_ip s_u s_c0 s_cv s_sl s_tx s_txe s_rt s_rte s_xsd s_st s_ste s_fs s_cb "
            "s_cbm s_E s_M s_xs s_yd s_yo s_y s_D s_pad").split())
        s_fso = sems("s_fso", 2)
        s_sub = sems("s_sub", 2)
        s_cst = sem("s_cst")
        s_cq = sems("s_cq", 2)
        s_z, s_zs, s_yz, s_yq, s_ryv, s_ryd, s_yt, s_yte = (
            sem(n) for n in "s_z s_zs s_yz s_yq s_ryv s_ryd s_yt s_yte".split())
        s_op2, s_om, s_xadd, s_out = sem("s_op2"), sem("s_om"), sem("s_xadd"), sem("s_out")
        UNITS = [(0, 1), (1, 4), (0, 2), (1, 3), (0, 3), (1, 2), (0, 0), (1, 0)]
        MASK = [T_UP, T_LOW]
        PAST_ = [T_GT, T_LT]

        def moe_sems():
            names = "logit score sel pos slot sc xt xtc gu silu act at atc dn ycopy np all".split()
            m = {n: sem(f"s_e_{n}") for n in names}
            for n in "lgu ldn lxg yst gat".split():
                m[n] = sems(f"s_e_{n}", 2)
            m["x2"], m["wa"], m["wg"] = sem("s_x2"), sem("s_wa"), sem("s_wg")
            return m

        ES = moe_sems()

        LED = {"pe": s_wused + [s_ip, s_yd, s_z, ES["at"]],
               "act": [s_zs, s_yq, ES["atc"], ES["ycopy"]] + s_fso + ES["yst"],
               "dve": [s_mcols, s_y, s_cbm, s_M, s_yz],
               "pool": [s_D]}

        LED2 = [ES["xt"], ES["gu"], ES["dn"]]

        block = ctx.enter_context(nc.Block())

        @block.sync
        def _(sp):
            sp.dma_start(tab[:, :], consts).then_inc(s_init, 16)
            sp.dma_start(ROWS0[0:KD, :], c_ctx.rearrange("(k p) -> k p", p=P)).then_inc(s_init, 16)
            sp.dma_start(ROWS0[KD:2 * KD, :], c[0, :].rearrange("(k p) -> k p", p=P)).then_inc(s_init, 16)
            sp.dma_start(ROWS0[2 * KD:2 * KD + 4 * MB_ROWS, :], mod_b.rearrange("l (b p) -> (l b) p", p=P)).then_inc(s_init, 16)
            sp.dma_start(ROWS0[2 * KD + 4 * MB_ROWS:P, :], norm1_g.rearrange("l (k p) -> (l k) p", p=P)).then_inc(s_init, 16)
            sp.dma_start(X[:, 0, :], x_prompt[0]).then_inc(s_x, 16)
            sp.dma_start(X[:, 1:NT, :], x_sample[0].rearrange("(t p) n -> p t n", p=P)).then_inc(s_x, 16)
            wv = [mod_w[l].rearrange("(k p) (b n) -> b p k n", p=P, n=512) for l in range(2)]
            with sp.Fori(0, 2) as i:
                for j in range(3):
                    sp.wait_ge(s_wused[j], i + 1)
                    sp.dma_start(WS[j], wv[0][i * 3 + j]).then_inc(s_w[j], 16)
            for j in range(3):
                sp.wait_ge(s_wused[j], 3)
                sp.dma_start(WS[j], w_qkv[0].rearrange("(k p) (j n) -> j p k n", p=P, j=3)[j]).then_inc(s_w[j], 16)
            sp.dma_start(gqk[:, 0, :], q_g.partition_broadcast(P)).then_inc(s_gqk, 16)
            sp.dma_start(gqk[:, 1, :], k_g.partition_broadcast(P)).then_inc(s_gqk, 16)
            sp.wait_ge(s_qkv, NT)
            wov = w_o[0].rearrange("(k p) (j n) -> j p k n", p=P, j=2)
            sp.dma_start(WS[1], wov[1]).then_inc(s_w[1], 16)
            for r0, rounds, l, b0 in ((0, 3, 0, 6), (3, 6, 1, 0)):
                with sp.Fori(0, rounds) as i:
                    for m, j in enumerate((0, 2)):
                        sp.wait_ge(s_wused[j], i + (r0 + 3))
                        sp.dma_start(WS[j], wv[l][i * 2 + (b0 + m)]).then_inc(s_w[j], 16)
            sp.wait_ge(s_wused[0], 12)
            sp.dma_start(WS[0], wov[0]).then_inc(s_w[0], 16)

            sp.wait_ge(s_zero, 1)
            sp.dma_start(xs_d.rearrange("(p a) (b n) -> p (a b) n", p=P, n=256),
                         zeros.unsqueeze(1).to_broadcast([P, MAXT * 4, 256])).then_inc(s_clear, 16)
            sp.dma_start(RW[:, :, :], router_w.rearrange("(k p) e -> p k e", p=P)).then_inc(s_rw, 16)
            sp.dma_start(RB[:, :], router_b.partition_broadcast(P)).then_inc(s_rw, 16)

            def expert_loads(l):
                sp.wait_ge(ES["np"], l + 1)
                done = 0 if l == 0 else sp.value_load(npi[0:1, 0:1], min_val=1, max_val=MAXT // 2)
                pairs = sp.value_load(npi[0:1, l:l + 1], min_val=1, max_val=MAXT // 2)
                if l == 0:
                    sp.wait_ge(s_op, NT)
                gv = w_gate[l].rearrange("e (k p) f -> e p k f", p=P)
                uv = w_up[l].rearrange("e (k p) f -> e p k f", p=P)
                dv = w_down[l].rearrange("e (k p) n -> e p k n", p=P)
                with sp.Fori(0, pairs) as i:
                    turn = i + done
                    e = [sp.value_load(eoti[0:1, bass.ds(i * 2 + j, 1)], min_val=0, max_val=NE - 1) for j in range(2)]
                    for j in range(2):
                        sp.wait_ge(ES["gu"], turn * 2 + j + 1)
                        sp.dma_start(WS[j][:, :, 0:FF], gv[e[j]]).then_inc(ES["lgu"][j], 16)
                        sp.dma_start(WS[j][:, :, FF:2 * FF], uv[e[j]]).then_inc(ES["lgu"][j], 16)
                        if j == 0:
                            sp.wait_ge(ES["sc"], 2 * NT * 16 * (l + 1))
                            for m in range(2):
                                sp.wait_ge(ES["xt"], turn * 2 + m + 1)
                                sp.dma_start(XG[m], xs_d.rearrange("(a p) n -> a p n", p=P)[i * 2 + m])\
                                    .then_inc(ES["lxg"][m], 16)
                    for j in range(2):
                        sp.wait_ge(ES["dn"], turn * 2 + j + 1)
                        sp.dma_start(WD[j], dv[e[j]]).then_inc(ES["ldn"][j], 16)

            expert_loads(0)

            ipv = in_proj[0].rearrange("(k p) n -> p k n", p=P)
            sp.wait_ge(s_ht, 3 * NT)
            sp.dma_start(CWR[0:5, :], conv_w[0]).then_inc(s_ssdin, 16)
            sp.dma_start(CWR[5:6, :], conv_b).then_inc(s_ssdin, 16)
            sp.dma_start(NGROWS, ssd_g[0].rearrange("(a n) -> a n", n=P)).then_inc(s_ssdin, 16)
            sp.dma_start(WDT, ipv[:, :, 2 * DI + 2 * SG * SN:2 * DI + 2 * SG * SN + 2 * SH]).then_inc(s_ssdin, 16)
            sp.dma_start(DTB, dt_bias[0].rearrange("d h -> (d h)").partition_broadcast(P)).then_inc(s_ssdin, 16)
            sp.dma_start(AROW, a_log[0].rearrange("d h -> (d h)").partition_broadcast(P)).then_inc(s_ssdin, 16)
            sp.dma_start(DROW, ssd_d[0].partition_broadcast(P)).then_inc(s_ssdin, 16)
            zv = ipv[:, :, 0:DI].rearrange("p k (c n) -> c p k n", c=SG)
            cv = cum_d.rearrange("(t d g h) q -> t d g (h q)", t=NT, d=2, g=SG)

            def sums_on_all(g, cc):
                for d in range(2):
                    sp.wait_ge(s_E, g * 10 + 2 * cc + d + 1)
                    sp.dma_start(RR[:, d].rearrange("p h n -> p (h n)"), cv[cc, d, g].partition_broadcast(P))\
                        .then_inc(s_cq[d], 16)

            sp.wait_ge(s_pre_dve, 4)
            sp.wait_ge(s_cst, 32)
            with sp.Fori(0, SG) as g:
                sp.wait_ge(s_ip, g * 6 + 1)
                for a in range(2):
                    sp.dma_start(WBC[:, :, a * P:(a + 1) * P],
                                 ipv[:, :, 2 * DI + a * SG * SN:2 * DI + (a + 1) * SG * SN]
                                 .rearrange("p k (g n) -> g p k n", g=SG)[g]).then_inc(s_wbc, 16)
                sp.wait_ge(s_z, g * 5 + 1)
                sp.dma_start(WX, ipv[:, :, DI:2 * DI].rearrange("p k (g n) -> g p k n", g=SG)[g]).then_inc(s_wx, 16)
                for d in range(2):
                    sp.wait_ge(s_fso[d], g * 16 + 1)
                    sp.dma_start(RAW[:, d], state_ssm[0, 0, d].rearrange("(g a b) q n -> g (b q) a n", g=SG, b=2)[g])\
                        .then_inc(s_raw, 16)
                sums_on_all(g, 0)
                sp.wait_ge(s_ip, (g + 1) * 6 + 1)
                for k in (KD // 2, 0):
                    sp.dma_start(WX[:, k:k + KD // 2, :], zv[g][:, k:k + KD // 2, :]).then_inc(s_wx, 16)
                for cc in range(1, NT):
                    sums_on_all(g, cc)
            ov = out_proj[0].rearrange("(b k p) (a n) -> a b p k n", b=2, p=P, a=2)
            sp.wait_ge(s_tx, SG * 5)
            sp.dma_start(WO[0][0], ov[0, 0]).then_inc(s_wbc, 16)
            sp.wait_ge(s_z, SG * 5 + 1)
            sp.dma_start(WO[0][1], ov[0, 1]).then_inc(s_w[0], 16)
            sp.wait_ge(s_yo, 4 * SG)
            sp.dma_start(WO[1][0], ov[1, 0]).then_inc(s_w[2], 16)
            sp.wait_ge(s_y, SG * NT + 1)
            sp.wait_ge(s_fso[0], SG * 16 + 1)
            sp.wait_ge(s_fso[1], SG * 16 + 1)
            sp.dma_start(WO[1][1], ov[1, 1]).then_inc(s_w[1], 16)
            sp.wait_ge(s_op2, 2 * NT)
            expert_loads(1)

        @block.tensor
        def _(pe):
            for s in LED["pe"]:
                pe.sem_inc(s, 1)
            for s in LED2:
                pe.sem_inc(s, 2)

            def norm_transposes(nn):
                for t in range(NT):
                    n = nn * NT + t
                    pe.wait_ge(s_h, n + 1)
                    if n >= 2:
                        pe.wait_ge(s_hT, n - 1)
                    for k in range(KD):
                        last = nc.tensor.transpose(psf[:, (n % 2) * 1024 + k * P:(n % 2) * 1024 + (k + 1) * P],
                                                   H[:, t, k * P:(k + 1) * P], ident)
                    last.then_inc(s_ht, 1)

            def mod_chunk(j, n):
                pe.wait_ge(s_mcols, n + 1)
                for k in range(KD):
                    last = nc.tensor.matmul(ps[0:2, 7, :], condT[:, :, k], WS[j][:, k, :], start=(k == 0), stop=(k == KD - 1))
                last.then_inc(s_wused[j], 1)

            def mod_turn(by_product):
                for m in range(4):
                    out, rows = ps[:, 7, 2 * m:2 * m + 2], MS[:, m * P:(m + 1) * P]
                    if by_product:
                        last = nc.tensor.matmul(out, rows, ident[0:2, 0:2], start=True, stop=True)
                    else:
                        last = nc.tensor.transpose(out, rows, ident[0:2, 0:2])
                last.then_inc(s_mturn, 1)

            def mod_rows(q0, q1, n):
                pe.wait_ge(s_mc, n)
                for cc in range(2):
                    last = nc.tensor.transpose(ps[0:(q1 - q0) * MB_ROWS, 6, cc * P:(cc + 1) * P],
                                               MODC[:, cc, q0 * MB_ROWS:q1 * MB_ROWS], ident)
                last.then_inc(s_mt, 1)

            pe.wait_ge(s_init, 80)
            nc.tensor.transpose(ps[:, 7, 0:P], ROWS0, ident).then_inc(s_condT, 1)
            norm_transposes(0)
            pe.wait_ge(s_condS, 1)
            with pe.Fori(0, 2) as i:
                for j in range(3):
                    pe.wait_ge(s_w[j], (i + 1) * 16)
                    mod_chunk(j, i * 3 + j)
                    pe.wait_ge(s_ms, i * 3 + (j + 1))
                    mod_turn(True)
            mod_rows(0, 1, 1)

            def turn_heads(t):
                src = [QF[:, 0:512], QF[:, 512:1024], KDUP[:, :, :, :].rearrange("p g two d -> p (g two d)")]
                if t == NT:
                    pe.wait_ge(s_kv, 48)
                    src = [KDC[:, :, :, :].rearrange("p g two d -> p (g two d)")]
                else:
                    pe.wait_ge(s_qf, t + 1)
                for r, s in enumerate(src):
                    m = 3 * t + r
                    if m >= 2:
                        pe.wait_ge(s_tqe, m - 1)
                    for a in range(4):
                        last = nc.tensor.transpose(ps[:, 6 + m % 2, a * P:(a + 1) * P], s[:, a * P:(a + 1) * P], ident)
                    last.then_inc(s_tq, 1)

            for j in range(3):
                pe.wait_ge(s_w[j], 3 * 16)
            pe.wait_ge(s_hT, NT)
            pe.wait_ge(s_apd, 1)
            pe.wait_ge(s_apa, 1)
            pe.wait_ge(s_mrow, 1)
            for t in range(NT):
                if t >= 2:
                    pe.wait_ge(s_qn, t - 1)
                    pe.wait_ge(s_v, t - 1)
                for j in range(3):
                    for k in range(KD):
                        last = nc.tensor.matmul(ps[:, 3 * (t % 2) + j, :], HT[:, k, t * P:(t + 1) * P], WS[j][:, k, :],
                                                start=(k == 0), stop=(k == KD - 1))
                last.then_inc(s_qkv, 1)
                if t >= 1:
                    turn_heads(t - 1)
            turn_heads(NT - 1)
            turn_heads(NT)

            def attend(T, k0, nk, chunks=()):
                def scores(h):
                    u = T * NH + h
                    b, half = h % 2, h % 2
                    if h == 0:
                        pe.wait_ge(s_qc, T + 1)
                    if not (isinstance(T, int) and T == 0 and h < 2):
                        pe.wait_ge(s_exp, u - 1)
                    q = QC[64 * half:64 * half + 64, h // 2, :]
                    kk = KT[64 * half:64 * half + 64, h // 4, :]
                    n = min(nk, 4) * P
                    last = nc.tensor.matmul(ps[:, 2 * b, 0:n], q, kk[:, k0 * P:k0 * P + n], start=True, stop=True)
                    if nk > 4:
                        last = nc.tensor.matmul(ps[:, 2 * b + 1, 0:P], q, kk[:, k0 * P + n:k0 * P + n + P],
                                                start=True, stop=True)
                    last.then_inc(s_S, 1)

                def turn(h):
                    u = T * NH + h
                    pe.wait_ge(s_exp, u + 1)
                    if not (isinstance(T, int) and T == 0 and h == 0):
                        pe.wait_ge(s_pte, u)
                    for j in range(nk):
                        last = nc.tensor.transpose(psf[:, 2048 + j * P:2048 + (j + 1) * P],
                                                   PR[h % 2][:, j * P:(j + 1) * P], ident)
                    last.then_inc(s_T, 1)

                def values(h):
                    u = T * NH + h
                    if h % 8 == 0 and not (isinstance(T, int) and T == 0 and h == 0):
                        pe.wait_ge(s_oev, 2 * T + h // 8)
                    pe.wait_ge(s_pte, u + 1)
                    for j in range(nk):
                        last = nc.tensor.matmul(ps[:, 6, (h % 8) * HD:(h % 8 + 1) * HD],
                                                PT[h % 2][:, j * P:(j + 1) * P],
                                                V[:, k0 + j, (h // 4) * HD:(h // 4 + 1) * HD],
                                                start=(j == 0), stop=(j == nk - 1))
                    last.then_inc(s_pv, 1)

                for s in range(NH + 2):
                    if chunks and s % 4 == 3:
                        pe.wait_ge(s_ms, i * 4 + (9 + s // 4))
                    if s < NH:
                        scores(s)
                    if 1 <= s <= NH:
                        turn(s - 1)
                    if s >= 2:
                        values(s - 2)
                    if chunks and s % 4 == 1 and s < NH:
                        m, j = s // 4, (0, 2)[s // 4 % 2]
                        pe.wait_ge(s_w[j], (i * 2 + (5 + m // 2)) * 16)
                        mod_chunk(j, i * 4 + (8 + m))
                    if chunks and s % 4 == 3:
                        mod_turn(False)

            pe.wait_ge(s_qn, NT)
            pe.wait_ge(s_v, NT)
            pe.wait_ge(s_tqe, 16)
            for n, j in enumerate((0, 2)):
                pe.wait_ge(s_w[j], 64)
                mod_chunk(j, 6 + n)
                pe.wait_ge(s_ms, 7 + n)
                mod_turn(True)
            attend(0, 0, 1)
            with pe.Fori(0, NT - 1) as i:
                attend(i + 1, 1, 5, True)

            pe.wait_ge(s_oev, 10)
            mod_rows(1, 4, 2)
            for s in range(NT + 1):
                if s < NT:
                    t = s
                    if t >= 2:
                        pe.wait_ge(s_otT, t - 1)
                    for k in range(KD):
                        last = nc.tensor.transpose(psf[:, (t % 2) * 1024 + k * P:(t % 2) * 1024 + (k + 1) * P],
                                                   OA[:, t, k * P:(k + 1) * P], ident)
                    last.then_inc(s_ot, 1)
                if s >= 1:
                    t = s - 1
                    pe.wait_ge(s_otT, t + 1)
                    if t == 0:
                        pe.wait_ge(s_w[0], 16 * 13)
                        pe.wait_ge(s_w[1], 16 * 4)
                    if t == 1:
                        pe.wait_ge(s_mrow, 2)
                    if t >= 2:
                        pe.wait_ge(s_opm, t - 1)
                    for j in range(2):
                        for k in range(KD):
                            last = nc.tensor.matmul(ps[:, 4 + 2 * (t % 2) + j, :], HT[:, k, t * P:(t + 1) * P],
                                                    WS[j][:, k, :], start=(k == 0), stop=(k == KD - 1))
                    last.then_inc(s_op, 1)

            def moe(l):
                nn = 2 * l + 1
                norm_transposes(nn)
                pe.wait_ge(s_rw, 32)
                for t in range(NT):
                    pe.wait_ge(s_hT, nn * NT + t + 1)
                    for k in range(KD):
                        last = nc.tensor.matmul(ps[:, 4, t * NE:(t + 1) * NE], HT[:, k, t * P:(t + 1) * P], RW[:, k, :],
                                                start=(k == 0), stop=(k == KD - 1))
                last.then_inc(ES["logit"], 1)
                pe.wait_ge(ES["sel"], l + 1)
                ones = tab[:, T_ONE:T_ONE + P]
                before = tab[:, T_LT:T_LT + P]
                for t in range(NT):
                    for a in range(t):
                        nc.tensor.matmul(ps[:, 5, t * NE:(t + 1) * NE], ones, chosen[:, a, :], start=(a == 0), stop=False)
                    nc.tensor.matmul(ps[:, 5, t * NE:(t + 1) * NE], before, chosen[:, t, :], start=(t == 0), stop=True)
                for t in range(NT):
                    last = nc.tensor.matmul(ps[:, 5, NT * NE:(NT + 1) * NE], ones, chosen[:, t, :], start=(t == 0), stop=(t == NT - 1))
                last.then_inc(ES["pos"], 1)

                pe.wait_ge(ES["np"], l + 1)
                done = 0 if l == 0 else pe.value_load(npi[0:1, 0:1], min_val=1, max_val=MAXT // 2)
                pairs = pe.value_load(npi[0:1, l:l + 1], min_val=1, max_val=MAXT // 2)
                pe.wait_ge(ES["slot"], l + 1)
                with pe.Fori(0, pairs) as i:
                    turn = i + done
                    for j in range(2):
                        pe.wait_ge(ES["lxg"][j], (turn + 1) * 16)
                        pe.wait_ge(ES["atc"], turn * 2 + 1)
                        for k in range(KD):
                            last = nc.tensor.transpose(psf[:, j * 1024 + k * P:j * 1024 + (k + 1) * P],
                                                       XG[j][:, k * P:(k + 1) * P], ident)
                        last.then_inc(ES["xt"], 1)
                    for j in range(2):
                        pe.wait_ge(ES["lgu"][j], (turn + 1) * 32)
                        pe.wait_ge(ES["xtc"], turn * 2 + j + 1)
                        pe.wait_ge(ES["ycopy"], turn * 2 + 1)
                        for k in range(KD):
                            last = nc.tensor.matmul(ps[:, 4 + j, :], XGT[j][:, k, :], WS[j][:, k, :],
                                                    start=(k == 0), stop=(k == KD - 1))
                        last.then_inc(ES["gu"], 1)
                    for j in range(2):
                        pe.wait_ge(ES["act"], turn * 2 + j + 1)
                        for k in range(2):
                            last = nc.tensor.transpose(psf[:, j * 1024 + k * P:j * 1024 + (k + 1) * P],
                                                       AC[j][:, k * P:(k + 1) * P], ident)
                        last.then_inc(ES["at"], 1)
                        pe.wait_ge(ES["atc"], turn * 2 + j + 2)
                        pe.wait_ge(ES["ldn"][j], (turn + 1) * 16)
                        if j == 1:
                            pe.wait_ge(ES["act"], turn * 2 + 2)
                        for n in range(2):
                            for k in range(2):
                                last = nc.tensor.matmul(ps[:, 6 - 2 * j + n, :], AT[j][:, k * P:(k + 1) * P], WD[j][:, k, n * 512:(n + 1) * 512],
                                                        start=(k == 0), stop=(k == 1))
                        last.then_inc(ES["dn"], 1)

            moe(0)
            norm_transposes(2)

            pe.wait_ge(s_ssdin, 112)
            for a in range(24):
                last = nc.tensor.transpose(ps[:, 7, a * 6:(a + 1) * 6], CWR[0:6, a * P:(a + 1) * P], ident[0:6, 0:6])
            nc.tensor.transpose(ps[:, 7, 144:160], NGROWS, ident[0:16, 0:16]).then_inc(s_pre_pe, 1)
            pe.wait_ge(s_ssdin, 112)
            for t in range(NT):
                if t == 0:
                    pe.wait_ge(s_hT, 3 * NT)
                    pe.wait_ge(s_apd, 2)
                    pe.wait_ge(s_apa, 2)
                for k in range(KD):
                    last = nc.tensor.matmul(ps[:, 6, t * 64:(t + 1) * 64], HT[:, k, t * P:(t + 1) * P], WDT[:, k, :],
                                            start=(k == 0), stop=(k == KD - 1))
            last.then_inc(s_pre_pe, 1)
            pe.wait_ge(s_pre_dve, 3)
            pe.wait_ge(s_pre_act, 1)
            for d in range(2):
                for bank, m in ((4, MASK[d]), (5, PAST_[d])):
                    nc.tensor.matmul(ps[:, bank, 0:320].rearrange("p (t d h) -> p t d h", t=NT, d=2)[:, :, d, :],
                                     tab[:, m:m + P], DA[:, :, d, :], start=True, stop=True)
            nc.tensor.matmul(ps[:, 7, 0:320], tab[:, T_ONE:T_ONE + P], DA.rearrange("p t d h -> p (t d h)"),
                             start=True, stop=True).then_inc(s_pre_pe, 1)

            pe.wait_ge(s_pre_act, 5)
            pe.wait_ge(s_hT, 3 * NT)
            cum = small[:, :]
            for a in range(3):
                w = min(P, NT * 2 * SH - a * P)
                last = nc.tensor.transpose(ps[0:w, 0, a * P:(a + 1) * P], cum[:, a * P:a * P + w], ident)
            last.then_inc(s_pre_pe, 1)

            pe.wait_ge(s_pre_act, 9)
            with pe.Fori(0, SG) as g:
                pe.wait_ge(s_zs, g * 5 + 1)
                for st in range(8):
                    if st < 6:
                        if st == 0:
                            pe.wait_ge(s_wbc, (g + 1) * 32)
                        if st == 2:
                            pe.wait_ge(s_wx, g * 48 + 16)
                        if st >= 2:
                            pe.wait_ge(s_u, g * 6 + st - 1)
                        b = 2 * (st % 2)
                        w = WBC[:, :, st * P:(st + 1) * P] if st < 2 else WX[:, :, (st - 2) * P:(st - 1) * P]
                        for k in range(KD):
                            nc.tensor.matmul(ps[:, b, :], w[:, k, :], HT[:, k, SEQ:TOK], start=(k == 0), stop=(k == KD - 1))
                        for k in range(KD):
                            last = nc.tensor.matmul(ps[:, b + 1, 0:SEQ], w[:, k, :], HT[:, k, 0:SEQ],
                                                    start=(k == 0), stop=(k == KD - 1))
                        last.then_inc(s_ip, 1)
                    if st == 2 or st >= 4:
                        a = st - 2
                        r = max(a - 1, 0)
                        pe.wait_ge(s_sl, g * 6 + a + 1)
                        if a == 0:
                            pe.wait_ge(s_y, g * 5 + 1)
                            pe.wait_ge(s_cbm, g * 5 + 1)
                        if r >= 1:
                            pe.wait_ge(s_txe, g * 5 + r)
                        src = CVT[a % 2] if a > 0 else BT
                        for t in range(NT):
                            last = nc.tensor.transpose(psf[:, 2048 + t * P:2048 + (t + 1) * P], src[:, t * P:(t + 1) * P], ident)
                        last.then_inc(s_tx, 1)
                pe.wait_ge(s_raw, (g + 1) * 32)
                for d in range(2):
                    for a in range(4):
                        last = nc.tensor.transpose(ps[:, 6 + d, a * P:(a + 1) * P], RAW[:, d, a, :], ident)
                    last.then_inc(s_rt, 1)
                pe.wait_ge(s_txe, (g + 1) * 5)
                for i, (d, cc) in enumerate(UNITS):
                    pe.wait_ge(s_xsd, g * 8 + i + 1)
                    if 2 <= i:
                        pe.wait_ge(s_ste, g * 6 + min(i - 1, 6))
                    xd = XD[:, d].rearrange("p h n -> p (h n)")
                    if cc > 0:
                        last = nc.tensor.matmul(ps[:, 4 + i % 2, :], BK[:, cc, :], xd, start=True, stop=True)
                    else:
                        for a in range(4):
                            last = nc.tensor.matmul(ps[:, 4 + i % 2, a * P:(a + 1) * P], xd[:, a * P:(a + 1) * P],
                                                    BK[:, 0, :], start=True, stop=True)
                    last.then_inc(s_st, 1)

                def c_times_b(cc):
                    if cc >= 1:
                        pe.wait_ge(s_cbm, g * 5 + cc + 1)
                    nc.tensor.matmul(ps[:, 5, 0:P], BT[:, cc * P:(cc + 1) * P], CT[:, cc * P:(cc + 1) * P],
                                     start=True, stop=True).then_inc(s_cb, 1)

                def gate_product(t):
                    if t == 0:
                        pe.wait_ge(s_wx, g * 48 + 48)
                    if t >= 4:
                        pe.wait_ge(s_zs, g * 5 + t - 2)
                    for k in range(KD):
                        last = nc.tensor.matmul(ps[:, t % 4, :], HT[:, k, t * P:(t + 1) * P], WX[:, k, :],
                                                start=(k == 0), stop=(k == KD - 1))
                    last.then_inc(s_z, 1)

                pe.wait_ge(s_u, (g + 1) * 6)
                pe.wait_ge(s_sl, (g + 1) * 6)
                pe.wait_ge(s_fs, (g + 1) * 2)
                c_times_b(0)
                gate_product(0)
                for cc in range(NT):
                    if cc + 1 < NT:
                        c_times_b(cc + 1)
                        gate_product(cc + 1)
                    if cc >= 1:
                        pe.wait_ge(s_y, g * 5 + cc + 1)
                        if cc == 1:
                            pe.wait_ge(s_rte, (g + 1) * 2)
                            pe.wait_ge(s_ste, (g + 1) * 6)
                        for d in range(2):
                            last = nc.tensor.matmul(ps[:, 6 + d, :], CT[:, cc * P:(cc + 1) * P], PV[:, d, cc - 1, :],
                                                    start=True, stop=True)
                        last.then_inc(s_yo, 1)
                    pe.wait_ge(s_xs, g * 5 + cc + 1)
                    pe.wait_ge(s_M, g * 5 + cc + 2)
                    for h in range(HG):
                        for d in range(2):
                            last = nc.tensor.matmul(ps[:, 4, h * SP:(h + 1) * SP], EE[:, d, h, :], XS[:, d, h, :],
                                                    start=(d == 0), stop=(d == 1))
                    last.then_inc(s_yd, 1)

            pe.wait_ge(s_zs, SG * NT + 1)
            for t in range(NT):
                for b in range(2):
                    n = 2 * t + b
                    pe.wait_ge(s_yz, 3 * NT + t + 2)
                    if n >= 2:
                        pe.wait_ge(s_yte, n - 1)
                    for k in range(KD):
                        last = nc.tensor.transpose(psf[:, b * 1024 + k * P:b * 1024 + (k + 1) * P],
                                                   Y[:, t, (b * KD + k) * P:(b * KD + k + 1) * P], ident)
                    last.then_inc(s_yt, 1)
            for a in range(2):
                if a == 0:
                    pe.wait_ge(s_wbc, 32 * SG + 16)
                    pe.wait_ge(s_w[0], 16 * 14)
                else:
                    pe.wait_ge(s_w[2], 16 * 13)
                    pe.wait_ge(s_w[1], 16 * 5)
                for t in range(NT):
                    n = a * NT + t
                    pe.wait_ge(s_yte, 2 * t + 2)
                    if n >= 4:
                        pe.wait_ge(s_om, n - 3)
                    if n == 0:
                        pe.wait_ge(s_y, SG * 5 + 1)
                    for b in range(2):
                        w = WO[a][b]
                        for k in range(KD):
                            last = nc.tensor.matmul(ps[:, 4 + n % 4, :], YT[b][:, k, t * P:(t + 1) * P], w[:, k, :],
                                                    start=(b == 0 and k == 0), stop=(b == 1 and k == KD - 1))
                    last.then_inc(s_op2, 1)
            moe(1)

        @block.scalar
        def _(act):
            for s in LED["act"]:
                act.sem_inc(s, 1)
            act.sem_inc(s_E, 2)
            order = Order(act, o_act)

            def norm_squares(nn):
                for t in range(NT):
                    if nn == 0:
                        act.wait_ge(s_x, 32)
                    order(nc.scalar.activation(SQX, X[:, t, :], ACT.Square, accum_out=ssq[:, t:t + 1]))
                nc.scalar.activation(ssq[:, 5:6], ssq[:, 0:1], ACT.Copy).then_inc(s_ss, 1)
                act.wait_ge(s_var, nn + 1)
                nc.scalar.activation(ssq[:, 0:NT], ssq[:, 0:NT], ACT.Sqrt).then_inc(s_sd, 1)

            def norm_columns(nn):
                for t in range(NT):
                    n = nn * NT + t
                    act.wait_ge(s_ht, n + 1)
                    nc.scalar.activation(HT[:, :, t * P:(t + 1) * P],
                                         psf[:, (n % 2) * 1024:(n % 2) * 1024 + 1024].rearrange("p (k n) -> p k n", k=KD),
                                         ACT.Copy).then_inc(s_hT, 1)

            def modulate(l):
                act.wait_ge(s_mc, l + 1)
                for k in range(KD // 2, KD):
                    for cc, (a, b) in enumerate(((0, SEQ), (SEQ, TOK))):
                        last = nc.scalar.activation(HT[:, k, a:b], HT[:, k, a:b], ACT.Identity,
                                                    scale=AB[:, l, 0, cc, k:k + 1], bias=AB[:, l, 1, cc, k:k + 1])
                last.then_inc(s_apa, 1)

            def mod_rows_out(q0, q1, n):
                act.wait_ge(s_mt, n)
                rows = (q1 - q0) * MB_ROWS
                nc.scalar.activation(MROW[0:rows], ps[0:rows, 6, 0:2 * P].rearrange("b (c n) -> b c n", c=2), ACT.Copy)\
                    .then_inc(s_mrow, 1)

            act.wait_ge(s_condT, 1)
            nc.scalar.activation(condT.rearrange("p c k -> p (c k)"), ps[:, 7, 0:16], ACT.Silu)
            nc.scalar.activation(COLS0, ps[:, 7, 0:P], ACT.Copy).then_inc(s_condS, 1)
            norm_squares(0)
            norm_columns(0)
            act.wait_ge(s_hT, NT)
            modulate(0)
            mod_rows_out(0, 1, 1)

            def head_columns(t):
                dst = [QT[:, 0:4, t * P:(t + 1) * P], QT[:, 4:8, t * P:(t + 1) * P], KT[:, :, t * P:(t + 1) * P]] \
                    if t < NT else [KT[:, :, t * P:(t + 1) * P]]
                for r, d in enumerate(dst):
                    m = 3 * t + r
                    act.wait_ge(s_tq, m + 1)
                    nc.scalar.activation(d, ps[:, 6 + m % 2, :].rearrange("p (a n) -> p a n", a=4), ACT.Copy)\
                        .then_inc(s_tqe, 1)

            for t in range(NT):
                b = 3 * (t % 2) * 512
                act.wait_ge(s_qkv, t + 1)
                nc.scalar.activation(SQ, psf[:, b:b + QK], ACT.Square).then_inc(s_sq, 1)
                nc.scalar.activation(V[:, t, :], psf[:, b + QK:b + QK + 256], ACT.Copy).then_inc(s_v, 1)
                act.wait_ge(s_varq, t + 1)
                nc.scalar.activation(rs[:, :], rs[:, :], ACT.Sqrt).then_inc(s_sdq, 1)
                if t >= 1:
                    head_columns(t - 1)
            head_columns(NT - 1)
            head_columns(NT)

            def probabilities(T, nk):
                for h in range(NH):
                    u = T * NH + h
                    act.wait_ge(s_max, u + 1)
                    if not (isinstance(T, int) and T == 0 and h < 2):
                        act.wait_ge(s_T, u - 1)
                    nc.scalar.activation(PR[h % 2][:, 0:nk * P], psf[:, 1024 * (h % 2):1024 * (h % 2) + nk * P],
                                         ACT.Exp, bias=nmx[:, h:h + 1], accum_out=den[:, h:h + 1]).then_inc(s_exp, 1)

            probabilities(0, 1)
            with act.Fori(0, NT - 1) as i:
                probabilities(i + 1, 5)
            act.wait_ge(s_modst[0], 16)
            mod_rows_out(1, 4, 2)

            for t in range(NT):
                act.wait_ge(s_ot, t + 1)
                nc.scalar.activation(HT[:, :, t * P:(t + 1) * P],
                                     psf[:, (t % 2) * 1024:(t % 2) * 1024 + 1024].rearrange("p (k n) -> p k n", k=KD),
                                     ACT.Copy).then_inc(s_otT, 1)

            def moe(l):
                nn = 2 * l + 1
                for t in range(NT):
                    act.wait_ge(s_x1, l * NT + t + 1)
                    order(nc.scalar.activation(SQX, X[:, t, :], ACT.Square, accum_out=ssq[:, t:t + 1]))
                nc.scalar.activation(ssq[:, 5:6], ssq[:, 0:1], ACT.Copy).then_inc(s_ss, 1)
                act.wait_ge(s_var, nn + 1)
                nc.scalar.activation(ssq[:, 0:NT], ssq[:, 0:NT], ACT.Sqrt).then_inc(s_sd, 1)
                norm_columns(nn)
                act.wait_ge(ES["logit"], l + 1)
                nc.scalar.activation(score, ps[:, 4, 0:NT * NE].rearrange("p (t e) -> p t e", t=NT), ACT.Sigmoid)\
                    .then_inc(ES["score"], 1)
                act.wait_ge(ES["np"], l + 1)
                done = 0 if l == 0 else act.value_load(npi[0:1, 0:1], min_val=1, max_val=MAXT // 2)
                pairs = act.value_load(npi[0:1, l:l + 1], min_val=1, max_val=MAXT // 2)
                with act.Fori(0, pairs) as i:
                    turn = i + done
                    for j in range(2):
                        act.wait_ge(ES["xt"], turn * 2 + j + 3)
                        nc.scalar.activation(XGT[j], psf[:, j * 1024:(j + 1) * 1024].rearrange("p (k n) -> p k n", k=KD),
                                             ACT.Copy).then_inc(ES["xtc"], 1)
                    for j in range(2):
                        act.wait_ge(ES["gu"], turn * 2 + j + 3)
                        nc.scalar.activation(SG_[j], ps[:, 4 + j, 0:FF], ACT.Silu).then_inc(ES["silu"], 1)
                    for j in range(2):
                        act.wait_ge(ES["at"], turn * 2 + j + 2)
                        nc.scalar.activation(AT[j], psf[:, j * 1024:j * 1024 + FF], ACT.Copy).then_inc(ES["atc"], 1)
                    for j in range(2):
                        act.wait_ge(ES["dn"], turn * 2 + j + 3)
                        act.wait_ge(ES["yst"][j], turn * 16 + 1)
                        nc.scalar.activation(YO[j], psf[:, (6 - 2 * j) * 512:(6 - 2 * j) * 512 + D], ACT.Copy)\
                            .then_inc(ES["ycopy"], 1)
                        act.wait_ge(ES["ycopy"], turn * 2 + j + 2)
                        act.dma_start(xs_d.rearrange("(a p) n -> a p n", p=P)[i * 2 + j], YO[j]).then_inc(ES["yst"][j], 16)
                for t in range(NT):
                    act.wait_ge(ES["gat"][t % 2], 32 * (t // 2 + 1 + l * (3 - t % 2)))
                    nc.scalar.activation(GY[t % 2][0], GY[t % 2][0], ACT.Copy, scale=gate2[:, 0, t:t + 1]).then_inc(ES["wa"], 1)

            moe(0)
            for t in range(NT):
                act.wait_ge(ES["x2"], t + 1)
                order(nc.scalar.activation(SQX, X[:, t, :], ACT.Square, accum_out=ssq[:, t:t + 1]))
            nc.scalar.activation(ssq[:, 5:6], ssq[:, 0:1], ACT.Copy).then_inc(s_ss, 1)
            act.wait_ge(s_var, 3)
            nc.scalar.activation(ssq[:, 0:NT], ssq[:, 0:NT], ACT.Sqrt).then_inc(s_sd, 1)
            norm_columns(2)
            act.wait_ge(s_hT, 3 * NT)
            modulate(1)

            act.wait_ge(s_pre_pe, 1)
            nc.scalar.activation(NGT, ps[:, 7, 144:160], ACT.Copy)
            nc.scalar.activation(CW, ps[:, 7, 0:144].rearrange("p (c j) -> p c j", j=6), ACT.Copy).then_inc(s_pre_act, 1)
            act.wait_ge(s_pre_dve, 1)
            nc.scalar.activation(sp1, sp1, ACT.Exp).then_inc(s_pre_act, 1)
            act.wait_ge(s_ssdin, 112)
            nc.scalar.activation(AROW, AROW, ACT.Exp).then_inc(s_pre_act, 1)
            act.wait_ge(s_pre_dve, 2)
            nc.scalar.activation(sp3, sp2, ACT.Ln).then_inc(s_pre_act, 1)
            act.wait_ge(s_pre_pe, 3)
            for i, dst in enumerate((CUM, EA, sp0, CD)):
                nc.scalar.activation(dst, ps[:, (4, 4, 5, 7)[i], 0:320].rearrange("p (t d h) -> p t d h", t=NT, d=2),
                                     ACT.Copy if i == 0 else ACT.Exp).then_inc(s_pre_act, 1)
            act.wait_ge(s_pre_pe, 4)
            nc.scalar.activation(CROWS[:, 0:2 * P], ps[:, 0, 0:2 * P], ACT.Copy)
            nc.scalar.activation(CROWS[0:64, 2 * P:], ps[0:64, 0, 2 * P:3 * P], ACT.Copy).then_inc(s_pre_act, 1)
            act.wait_ge(s_pre_act, 9)
            act.dma_start(cum_d[0:2 * P].rearrange("(a r) q -> r a q", a=2), CROWS[:, 0:2 * P].rearrange("r (a q) -> r a q", a=2))\
                .then_inc(s_cst, 16)
            act.dma_start(cum_d[2 * P:], CROWS[0:64, 2 * P:]).then_inc(s_cst, 16)
            act.wait_ge(s_pad, 1)
            with act.Fori(0, SG) as g:
                act.wait_ge(s_D, g * 5 + 1)
                for st in range(9):
                    if st < 6:
                        b = 1024 * (st % 2)
                        act.wait_ge(s_ip, g * 6 + st + 2)
                        nc.scalar.activation(U[st % 2][:, 2:2 + DEC], psf[:, b:b + DEC], ACT.Copy).then_inc(o_u, 1)
                        nc.scalar.activation(U[st % 2][:, 4 + DEC:4 + DEC + SEQ], psf[:, b + 512:b + 512 + SEQ], ACT.Copy)\
                            .then_inc(s_u, 1)
                        act.wait_ge(s_u, g * 6 + st + 1)
                        act.wait_ge(o_u, g * 6 + st + 1)
                        ch = (g + 16 + 4 * st) if st < 2 else (g * 4 + st - 2)
                        nc.scalar.activation(AC2[st % 2], U[st % 2][:, 2:2 + AW], ACT.Identity,
                                             scale=CW[:, bass.ds(ch, 1), 2:3].rearrange("p a b -> p (a b)"),
                                             bias=CW[:, bass.ds(ch, 1), 5:6].rearrange("p a b -> p (a b)")).then_inc(s_c0, 1)
                    if 1 <= st <= 6:
                        a = st - 1
                        act.wait_ge(s_cv, g * 6 + a + 1)
                        if 4 <= a:
                            act.wait_ge(s_tx, g * 5 + a - 2)
                        dst = (BT, CT)[a] if a < 2 else CVT[a % 2]
                        nc.scalar.activation(dst[:, SEQ:TOK], AC2[a % 2][:, 0:DEC], ACT.Silu)
                        nc.scalar.activation(dst[:, 0:SEQ], AC2[a % 2][:, DEC + 2:DEC + 2 + SEQ], ACT.Silu).then_inc(s_sl, 1)
                    if st == 3 or 5 <= st:
                        a = st - 3
                        act.wait_ge(s_tx, g * 5 + max(a - 1, 0) + 1)
                        dst = XT[:, :, (a - 2) * P:(a - 1) * P] if a > 0 else BK
                        nc.scalar.activation(dst, psf[:, 2048:2048 + TOK].rearrange("p (t n) -> p t n", t=NT), ACT.Copy)\
                            .then_inc(s_txe, 1)
                for d in range(2):
                    act.wait_ge(s_rt, g * 2 + d + 1)
                    nc.scalar.activation(PV[:, d, 3 * d, :], ps[:, 6 + d, :], ACT.Copy).then_inc(s_rte, 1)
                for d in range(2):
                    act.wait_ge(s_st, g * 8 + 7 + d)
                    nc.scalar.activation(RAW[:, d].rearrange("p a n -> p (a n)"), ps[:, 4 + d, :], ACT.Copy).then_inc(s_fs, 1)
                for d in range(2):
                    act.wait_ge(s_fs, g * 2 + 1 + d)
                    act.dma_start(new_ssm[0, 0, d].rearrange("(g a b) q n -> g (b q) a n", g=SG, b=2)[g], RAW[:, d])\
                        .then_inc(s_fso[d], 16)

                def square(t):
                    act.wait_ge(s_yz, g * 5 + t + 2)
                    act.wait_ge(s_yq, g * 5 + t + 1)
                    nc.scalar.activation(ZS[t % 2], Y[:, t, bass.ds(g * 512, 512)], ACT.Square,
                                         accum_out=ssy[:, t, bass.ds(g, 1)]).then_inc(s_yq, 1)

                for cc in range(NT):
                    act.wait_ge(s_yd, g * 5 + cc + 1)
                    for d, ready in enumerate(s_sub):
                        act.wait_ge(ready, g * 5 + cc + 1)
                        nc.scalar.activation(EE[:, d], RR[:, d], ACT.Exp).then_inc(s_E, 1)
                    act.wait_ge(s_z, g * 5 + cc + 2)
                    act.wait_ge(s_yq, g * 5 + max(cc - 1, 0) + 1)
                    nc.scalar.activation(ZS[cc % 2], ps[:, cc % 4, :], ACT.Silu).then_inc(s_zs, 1)
                    if cc >= 1:
                        square(cc - 1)
                square(NT - 1)
            act.wait_ge(s_ryv, 1)
            nc.scalar.activation(ry[:, :], ry[:, :], ACT.Sqrt).then_inc(s_ryd, 1)
            moe(1)

        @block.vector
        def _(dve):
            for s in LED["dve"]:
                dve.sem_inc(s, 1)
            order = Order(dve, o_dve)

            def norm_rows(nn):
                half = nn % 2
                dve.wait_ge(s_mb[nn], 48)
                for cc in range(2):
                    order(nc.vector.scalar_tensor_tensor(MB[half][:, 1, cc, :], MB[half][:, 1, cc, :], 1.0, G,
                                                         op0=ALU.add, op1=ALU.mult))
                dve.wait_ge(s_ss, nn + 1)
                nc.vector.tensor_scalar(ssq[:, 0:NT], ssq[:, 0:NT], 1.0 / D, EPS, ALU.mult, ALU.add).then_inc(s_var, 1)
                dve.wait_ge(s_sd, nn + 1)
                order(nc.vector.reciprocal(ssq[:, 0:NT], ssq[:, 0:NT]))
                for t in range(NT):
                    nc.vector.scalar_tensor_tensor(H[:, t, :], X[:, t, :], ssq[:, t:t + 1],
                                                   MB[half][:, 1, min(t, 1), :],
                                                   op0=ALU.mult, op1=ALU.mult).then_inc(s_hm, 1)

            def norm_plain(nn):
                dve.wait_ge(s_ss, nn + 1)
                nc.vector.tensor_scalar(ssq[:, 0:NT], ssq[:, 0:NT], 1.0 / D, EPS, ALU.mult, ALU.add).then_inc(s_var, 1)
                dve.wait_ge(s_sd, nn + 1)
                order(nc.vector.reciprocal(ssq[:, 0:NT], ssq[:, 0:NT]))
                for t in range(NT):
                    nc.vector.tensor_scalar(H[:, t, :], X[:, t, :], ssq[:, t:t + 1], None, ALU.mult).then_inc(s_h, 1)

            def mod_product(j, n, used):
                dve.wait_ge(s_wused[j], used)
                nc.vector.tensor_copy(MS, ps[0:2, 7, :]).then_inc(s_ms, 1)

            def mod_columns(n):
                dve.wait_ge(s_mturn, n + 1)
                nc.vector.tensor_tensor(MODC[:, :, bass.ds(n * 4, 4)], ps[:, 7, 0:8].rearrange("p (b c) -> p c b", c=2),
                                        bias_cols[:, bass.ds(n * 4, 4)].unsqueeze(1).to_broadcast([P, 2, 4]), ALU.add)\
                    .then_inc(s_mcols, 1)

            def factors(l):
                first = 2 * l * MB_ROWS
                dve.wait_ge(s_mcols, (6, 24)[l] + 1)
                for cc in range(2):
                    nc.vector.scalar_tensor_tensor(AB[:, l, 0, cc, :], MODC[:, cc, first + KD:first + 2 * KD], 1.0, g1_cols[:, l],
                                                   op0=ALU.add, op1=ALU.mult)
                    last = nc.vector.tensor_copy(AB[:, l, 1, cc, :], MODC[:, cc, first:first + KD])
                last.then_inc(s_mc, 1)

            def modulate(l):
                dve.wait_ge(s_mc, l + 1)
                dve.wait_ge(s_hT, (2 * l + 1) * NT)
                for k in range(KD // 2):
                    for cc, (a, b) in enumerate(((0, SEQ), (SEQ, TOK))):
                        last = nc.vector.tensor_scalar(HT[:, k, a:b], HT[:, k, a:b], AB[:, l, 0, cc, k:k + 1],
                                                       AB[:, l, 1, cc, k:k + 1], ALU.mult, ALU.add)
                last.then_inc(s_apd, 1)

            dve.wait_ge(s_x, 32)
            norm_plain(0)
            dve.wait_ge(s_condS, 1)
            with dve.Fori(0, 2) as i:
                for j in range(3):
                    mod_product(j, i * 3 + j, i + 2)
                    mod_columns(i * 3 + j)
            factors(0)
            modulate(0)

            dve.wait_ge(s_gqk, 32)
            for t in range(NT):
                b = 3 * (t % 2) * 512
                dve.wait_ge(s_sq, t + 1)
                order(nc.vector.tensor_reduce(rs[:, :], SQ.rearrange("p (h d) -> p h d", d=HD), AX.X, ALU.add))
                nc.vector.tensor_scalar(rs[:, :], rs[:, :], 1.0 / HD, EPS, ALU.mult, ALU.add).then_inc(s_varq, 1)
                dve.wait_ge(s_sdq, t + 1)
                order(nc.vector.reciprocal(rs[:, :], rs[:, :]))
                order(nc.vector.tensor_scalar(rs[:, 0:NH], rs[:, 0:NH], HD ** -0.5, None, ALU.mult))
                if t == 1:
                    dve.wait_ge(s_qf, 1)
                nc.vector.tensor_tensor(QN.rearrange("p (h d) -> p h d", d=HD),
                                        psf[:, b:b + QK].rearrange("p (h d) -> p h d", d=HD),
                                        rs[:, :].unsqueeze(2).to_broadcast([P, NH + NKV, HD]), ALU.mult).then_inc(s_qn, 1)
                dve.wait_ge(s_qg, t + 1)
                if t >= 1:
                    dve.wait_ge(s_t2, t)
                    cos = tab[:, T_COS + (t - 1) * HD:T_COS + t * HD].unsqueeze(1).to_broadcast([P, NH + NKV, HD])
                    order(nc.vector.tensor_tensor(QN.rearrange("p (h d) -> p h d", d=HD),
                                                  QN.rearrange("p (h d) -> p h d", d=HD), cos, ALU.mult))
                    dve.wait_ge(s_tq, 3 * t)
                    nc.vector.tensor_tensor(QF, QN[:, 0:D], T2[:, 0:D], ALU.add)
                    nc.vector.tensor_tensor(KDUP,
                                            QN[:, D:QK].rearrange("p (g d) -> p g d", d=HD).unsqueeze(2).to_broadcast([P, NKV, 2, HD]),
                                            T2[:, D:QK].rearrange("p (g d) -> p g d", d=HD).unsqueeze(2).to_broadcast([P, NKV, 2, HD]),
                                            ALU.add).then_inc(s_qf, 1)
                else:
                    nc.vector.tensor_copy(QF, QN[:, 0:D])
                    nc.vector.tensor_copy(KOUT, QN[:, D:QK])
                    nc.vector.tensor_copy(KDUP, QN[:, D:QK].rearrange("p (g d) -> p g d", d=HD)
                                          .unsqueeze(2).to_broadcast([P, NKV, 2, HD])).then_inc(s_qf, 1)

            def softmax_parts(T, nk, chunks=False):
                def row_max(h):
                    dve.wait_ge(s_S, T * NH + h + 1)
                    nc.vector.tensor_reduce(nmx[:, h:h + 1], psf[:, 1024 * (h % 2):1024 * (h % 2) + nk * P],
                                            AX.X, ALU.max, negate=True).then_inc(s_max, 1)

                def turned(h):
                    u = T * NH + h
                    dve.wait_ge(s_T, u + 1)
                    if not (isinstance(T, int) and T == 0 and h < 2):
                        dve.wait_ge(s_pv, u - 1)
                    nc.vector.tensor_copy(PT[h % 2][:, 0:nk * P], psf[:, 2048:2048 + nk * P]).then_inc(s_pte, 1)

                def normed(half):
                    dve.wait_ge(s_pv, T * NH + 8 * half + 8)
                    hs = slice(8 * half, 8 * half + 8)
                    nc.vector.reciprocal(rden[:, hs], den[:, hs]).then_inc(o_rden, 1)
                    dve.wait_ge(o_rden, 2 * T + half + 1)
                    nc.vector.tensor_tensor(
                        OA[:, T, 512 * half:512 * half + 512].rearrange("p (h d) -> p h d", d=HD),
                        ps[:, 6, :].rearrange("p (h d) -> p h d", d=HD),
                        rden[:, hs].unsqueeze(2).to_broadcast([P, 8, HD]), ALU.mult).then_inc(s_oev, 1)

                for s in range(NH + 1):
                    if s < NH:
                        row_max(s)
                    if s >= 1:
                        turned(s - 1)
                    if s == 9:
                        normed(0)
                    if chunks and s % 4 == 2:
                        m, j = s // 4, (0, 2)[s // 4 % 2]
                        mod_product(j, i * 4 + (8 + m), i * 2 + (5 + m // 2))
                    if chunks and s % 4 == 0 and s > 0:
                        mod_columns(i * 4 + (7 + s // 4))
                normed(1)

            for n, j in enumerate((0, 2)):
                mod_product(j, 6 + n, 4)
                mod_columns(6 + n)
            softmax_parts(0, 1)
            with dve.Fori(0, NT - 1) as i:
                softmax_parts(i + 1, 5, True)

            factors(1)
            dve.wait_ge(s_mb[0], 16)
            for t in range(NT):
                dve.wait_ge(s_op, t + 1)
                b = 2048 + 1024 * (t % 2)
                if t >= 1:
                    dve.wait_ge(s_x1, t)
                nc.vector.tensor_tensor(JUNK, psf[:, b:b + D], MB[0][:, 2, min(t, 1), :], ALU.mult).then_inc(s_opm, 1)

            def moe(l):
                nn = 2 * l + 1
                norm_rows(nn)
                V_ = nc.vector
                dve.wait_ge(ES["score"], l + 1)
                dve.wait_ge(s_rw, 32)
                order(V_.tensor_tensor(biased, score, RB[:, :].unsqueeze(1).to_broadcast([P, NT, NE]), ALU.add))
                bv = biased.rearrange("p t (g e) -> p (t g) e", g=NG)
                other = bv.unsqueeze(2).to_broadcast([P, NT * NG, EG, EG])
                own = bv.unsqueeze(3).to_broadcast([P, NT * NG, EG, EG])
                tie = tab[:, T_TIE:T_END].rearrange("p (e f) -> p e f", e=EG).unsqueeze(1)
                V_.tensor_tensor(above, other, own, ALU.is_gt)
                order(V_.tensor_tensor(equal, other, own, ALU.is_equal))
                order(V_.tensor_tensor(equal, equal, tie.to_broadcast([P, NT * NG, EG, EG]), ALU.mult))
                order(V_.tensor_tensor(above, above, equal, ALU.add))
                cv = chosen.rearrange("p t (g e) -> p (t g) e", g=NG)
                order(V_.tensor_reduce(cv, above, AX.X, ALU.add))
                order(V_.tensor_scalar(chosen, chosen, 1.5, None, ALU.is_lt))
                order(V_.tensor_tensor(weighted, chosen, biased, ALU.mult))
                order(V_.tensor_reduce(gsum.rearrange("p t g -> p (t g)"), weighted.rearrange("p t (g e) -> p (t g) e", g=NG),
                                       AX.X, ALU.add))
                ga, ge = above[:, 0:NT], equal[:, 0:NT]
                other = gsum.unsqueeze(2).to_broadcast([P, NT, NG, NG])
                own = gsum.unsqueeze(3).to_broadcast([P, NT, NG, NG])
                V_.tensor_tensor(ga, other, own, ALU.is_gt)
                order(V_.tensor_tensor(ge, other, own, ALU.is_equal))
                order(V_.tensor_tensor(ge, ge, tie.to_broadcast([P, NT, NG, NG]), ALU.mult))
                order(V_.tensor_tensor(ga, ga, ge, ALU.add))
                order(V_.tensor_reduce(gtop, ga, AX.X, ALU.add))
                order(V_.tensor_scalar(gtop, gtop, 0.5, None, ALU.is_lt))
                gt = gtop.rearrange("p t g -> p (t g)").unsqueeze(2).to_broadcast([P, NT * NG, EG])
                V_.tensor_tensor(cv, cv, gt, ALU.mult).then_inc(ES["sel"], 1)
                dve.wait_ge(ES["sel"], l + 1)
                order(V_.tensor_tensor(weighted, chosen, score, ALU.mult))
                order(V_.tensor_reduce(wsum, weighted, AX.X, ALU.add))
                order(V_.reciprocal(wsum, wsum))
                order(V_.tensor_tensor(weighted, weighted, wsum.unsqueeze(2).to_broadcast([P, NT, NE]), ALU.mult))
                order(V_.tensor_scalar(steps, tab[:, T_IOTA:T_IOTA + MAXT], float(P), None, ALU.mult))
                dve.wait_ge(ES["pos"], l + 1)
                V_.tensor_copy(place, ps[:, 5, 0:NT * NE].rearrange("p (t e) -> p t e", t=NT))
                order(V_.tensor_copy(count, ps[:, 5, NT * NE:(NT + 1) * NE]))
                order(V_.tensor_tensor(full, count.unsqueeze(2).to_broadcast([P, NE, NT]),
                                       steps[:, 0:NT].unsqueeze(1).to_broadcast([P, NE, NT]), ALU.is_gt))
                order(V_.tensor_reduce(tiles_of, full, AX.X, ALU.add))
                order(V_.tensor_tensor_scan(upto, tab[:, T_ONE:T_ONE + NE], tiles_of, 0.0, ALU.mult, ALU.add))
                order(V_.tensor_scalar(steps[0:1, :], tab[0:1, T_IOTA:T_IOTA + MAXT], 2.0, None, ALU.mult))
                order(V_.tensor_scalar(steps[0:1, :], steps[0:1, :], upto[0:1, NE - 1:NE], None, ALU.is_lt))
                order(V_.tensor_reduce(npf[:, :], steps[0:1, :], AX.X, ALU.add))
                V_.tensor_copy(npi[:, l:l + 1], npf[:, :])
                order(V_.tensor_tensor(ended[0:1], upto[0:1].unsqueeze(1).to_broadcast([1, MAXT, NE]),
                                       tab[0:1, T_IOTA:T_IOTA + MAXT].unsqueeze(2).to_broadcast([1, MAXT, NE]), ALU.is_le))
                order(V_.tensor_reduce(eotf[:, :], ended[0:1], AX.X, ALU.add))
                order(V_.tensor_scalar(eotf[:, :], eotf[:, :], NE - 1.0, None, ALU.min))
                V_.tensor_copy(eoti[:, :], eotf[:, :]).then_inc(ES["np"], 1)
                order(V_.tensor_tensor(base, upto, tiles_of, ALU.subtract))
                order(V_.tensor_scalar(base, base, float(P), 1.0, ALU.mult, ALU.add))
                order(V_.tensor_tensor(spot, place, base.unsqueeze(1).to_broadcast([P, NT, NE]), ALU.add))
                order(V_.tensor_tensor(spot, spot, chosen, ALU.mult))
                order(V_.tensor_reduce(slotf[:, 0, :], spot, AX.X, ALU.max))
                order(V_.tensor_reduce(tot, spot, AX.X, ALU.add))
                order(V_.tensor_tensor(slotf[:, 1, :], tot, slotf[:, 0, :], ALU.subtract))
                for a in range(2):
                    order(V_.tensor_tensor(mine, spot, slotf[:, a, :].unsqueeze(2).to_broadcast([P, NT, NE]), ALU.is_equal))
                    order(V_.tensor_tensor(mine, mine, weighted, ALU.mult))
                    order(V_.tensor_reduce(gate2[:, a, :], mine, AX.X, ALU.add))
                order(V_.tensor_scalar(slotf[:, :, :], slotf[:, :, :], 1.0, None, ALU.subtract))
                V_.tensor_copy(sloti[:, :, :], slotf[:, :, :]).then_inc(ES["slot"], 1)

                dve.wait_ge(ES["np"], l + 1)
                done = 0 if l == 0 else dve.value_load(npi[0:1, 0:1], min_val=1, max_val=MAXT // 2)
                pairs = dve.value_load(npi[0:1, l:l + 1], min_val=1, max_val=MAXT // 2)
                with dve.Fori(0, pairs) as i:
                    turn = i + done
                    for j in range(2):
                        dve.wait_ge(ES["silu"], turn * 2 + j + 1)
                        dve.wait_ge(ES["at"], turn * 2 + 1)
                        V_.tensor_tensor(AC[j], ps[:, 4 + j, FF:2 * FF], SG_[j], ALU.mult).then_inc(ES["act"], 1)
                for t in range(NT):
                    a, b = GY[t % 2]
                    dve.wait_ge(ES["wa"], l * NT + t + 1)
                    order(V_.scalar_tensor_tensor(b, b, gate2[:, 1, t:t + 1], a, op0=ALU.mult, op1=ALU.add))
                    V_.tensor_tensor(b, b, MB[1][:, 2, min(t, 1), :], ALU.mult).then_inc(ES["wg"], 1)

            moe(0)
            norm_plain(2)
            modulate(1)
            V_ = nc.vector
            dve.wait_ge(s_pre_pe, 2)
            dve.wait_ge(s_ssdin, 112)
            dve.wait_ge(s_pre_act, 1)
            bias = DTB.rearrange("p (d h) -> p d h", d=2).unsqueeze(1).to_broadcast([P, NT, 2, SH])
            order(V_.tensor_tensor(sp0, ps[:, 6, 0:320].rearrange("p (t d h) -> p t d h", t=NT, d=2), bias, ALU.add))
            order(V_.tensor_scalar(sp1, sp0, -1.0, None, ALU.mult))
            V_.tensor_tensor(sp1, sp1, sp0, ALU.min).then_inc(s_pre_dve, 1)
            dve.wait_ge(s_pre_act, 2)
            V_.tensor_scalar(sp2, sp1, 1.0, None, ALU.add).then_inc(s_pre_dve, 1)
            dve.wait_ge(s_pre_dve, 2)
            dve.wait_ge(s_pre_act, 4)
            order(V_.tensor_scalar(sp2, sp2, 1.0, None, ALU.subtract))
            order(V_.tensor_scalar(sp4, sp2, 0.0, None, ALU.is_equal))
            V_.tensor_tensor(sp3, sp3, sp4, ALU.add)
            order(V_.tensor_tensor(sp2, sp2, sp4, ALU.add))
            order(V_.reciprocal(sp2, sp2))
            order(V_.tensor_tensor(sp3, sp3, sp1, ALU.mult))
            order(V_.tensor_tensor(sp3, sp3, sp2, ALU.mult))
            order(V_.tensor_scalar(sp0, sp0, 0.0, None, ALU.max))
            order(V_.tensor_tensor(DTA, sp0, sp3, ALU.add))
            dve.wait_ge(s_pre_act, 3)
            am = AROW.rearrange("p (d h) -> p d h", d=2).unsqueeze(1).to_broadcast([P, NT, 2, SH])
            order(V_.tensor_tensor(DA, DTA, am, ALU.mult))
            V_.tensor_scalar(DA, DA, -1.0, None, ALU.mult).then_inc(s_pre_dve, 1)
            dve.wait_ge(s_pre_act, 7)
            V_.tensor_tensor(DTD, DTA, sp0, ALU.mult).then_inc(s_pre_dve, 1)
            dve.wait_ge(s_pre_dve, 4)

            dve.wait_ge(s_ssdin, 112)
            with dve.Fori(0, SG) as g:
                heads = bass.ds(g * HG, HG)
                for st in range(6):
                    ch = (g + 16 + 4 * st) if st < 2 else (g * 4 + st - 2)
                    dve.wait_ge(s_c0, g * 6 + st + 1)
                    for i, j in enumerate((0, 1, 3, 4)):
                        x = V_.scalar_tensor_tensor(AC2[st % 2], U[st % 2][:, j:j + AW],
                                                    CW[:, bass.ds(ch, 1), j:j + 1].rearrange("p a b -> p (a b)"), AC2[st % 2],
                                                    op0=ALU.mult, op1=ALU.add)
                        if i < 3:
                            x.then_inc(o_cv, 1)
                            dve.wait_ge(o_cv, g * 18 + 3 * st + i + 1)
                    x.then_inc(s_cv, 1)
                for i, (d, cc) in enumerate(UNITS[:6]):
                    src, dst = (cc - 1, cc) if d == 0 else (cc - 1, cc - 2)
                    if i < 2:
                        dve.wait_ge(s_rte, g * 2 + d + 1)
                    if i >= 2:
                        dve.wait_ge(s_ste, g * 6 + i - 1)
                    V_.tensor_tensor(PV[:, d, dst, :].rearrange("p (h n) -> p h n", h=HG),
                                     PV[:, d, src, :].rearrange("p (h n) -> p h n", h=HG),
                                     CD[:, cc, d, heads].unsqueeze(2).to_broadcast([P, HG, SP]), ALU.mult).then_inc(o_pv, 1)
                    dve.wait_ge(o_pv, g * 6 + i + 1)
                    dve.wait_ge(s_st, g * 8 + i + 1)
                    V_.tensor_tensor(PV[:, d, dst, :], PV[:, d, dst, :], ps[:, 4 + i % 2, :], ALU.add).then_inc(s_ste, 1)

                def cb_masked(cc):
                    dve.wait_ge(s_cb, g * 5 + cc + 1)
                    dve.wait_ge(s_M, g * 5 + cc + 1)
                    for d in range(2):
                        x = V_.tensor_tensor(CB[:, d, :], ps[:, 5, 0:P], tab[:, MASK[d]:MASK[d] + P], ALU.mult)
                    x.then_inc(s_cbm, 1)

                def sums_between(cc):
                    for d in range(2):
                        dve.wait_ge(s_cq[d], (g * 5 + cc + 1) * 16)
                        for h in range(HG):
                            x = V_.tensor_scalar(RR[:, d, h, :], RR[:, d, h, :],
                                                 CUM[:, cc, d, bass.ds(g * HG + h, 1)], 0.0, ALU.subtract, ALU.min)
                        x.then_inc(s_sub[d], 1)

                def weights(cc):
                    dve.wait_ge(s_cbm, g * 5 + cc + 2)
                    for d in range(2):
                        dve.wait_ge(s_E, g * 10 + 2 * cc + d + 3)
                        x = V_.tensor_tensor(EE[:, d], EE[:, d], CB[:, d, :].unsqueeze(1).to_broadcast([P, HG, P]), ALU.mult)
                    x.then_inc(s_M, 1)

                def add_up(cc):
                    y = Y[:, cc, bass.ds(g * 512, 512)]
                    yh = y.rearrange("p (h n) -> p h n", h=HG)
                    dve.wait_ge(s_D, g * 5 + cc + 2)
                    dve.wait_ge(s_yd, g * 5 + cc + 2)
                    k = 0
                    if cc >= 1:
                        dve.wait_ge(s_yo, g * 4 + cc)
                        for d in range(2):
                            th = ps[:, 6 + d, :].rearrange("p (h n) -> p h n", h=HG)
                            V_.tensor_tensor(th, th,
                                             EA[:, cc, d, heads].unsqueeze(2).to_broadcast([P, HG, SP]), ALU.mult).then_inc(o_y, 1)
                            dve.wait_ge(o_y, g * 16 + 4 * (cc - 1) + 2 * d + 1)
                            V_.tensor_tensor(y, y, ps[:, 6 + d, :], ALU.add).then_inc(o_y, 1)
                            dve.wait_ge(o_y, g * 16 + 4 * (cc - 1) + 2 * d + 2)
                    V_.tensor_tensor(y, y, ps[:, 4, :], ALU.add).then_inc(s_y, 1)
                    dve.wait_ge(s_y, g * 5 + cc + 2)
                    dve.wait_ge(s_zs, g * 5 + cc + 2)
                    V_.tensor_tensor(y, y, ZS[cc % 2], ALU.mult).then_inc(s_yz, 1)

                sums_between(0)
                for cc in range(NT):
                    cb_masked(cc)
                    if cc >= 1:
                        add_up(cc - 1)
                    weights(cc)
                    if cc + 1 < NT:
                        sums_between(cc + 1)
                add_up(NT - 1)

            dve.wait_ge(s_yq, SG * NT + 1)
            order(V_.tensor_reduce(ry[:, :], ssy[:, :, :], AX.X, ALU.add))
            V_.tensor_scalar(ry[:, :], ry[:, :], 1.0 / DI, EPS, ALU.mult, ALU.add).then_inc(s_ryv, 1)
            dve.wait_ge(s_D, SG * NT + 1)
            dve.wait_ge(s_ryd, 1)
            order(V_.reciprocal(ry[:, :], ry[:, :]))
            for n in range(2 * NT):
                t, b = n // 2, n % 2
                dve.wait_ge(s_yt, n + 1)
                V_.tensor_tensor(YT[b][:, :, t * P:(t + 1) * P],
                                 psf[:, b * 1024:b * 1024 + 1024].rearrange("p (k n) -> p k n", k=KD),
                                 NGT[:, b * KD:(b + 1) * KD].unsqueeze(2).to_broadcast([P, KD, P]), ALU.mult)\
                    .then_inc(s_yte, 1)
            dve.wait_ge(s_mb[2], 16)
            for n in range(2 * NT):
                a, t = n // NT, n % NT
                dve.wait_ge(s_op2, n + 1)
                if n >= 2:
                    dve.wait_ge(s_xadd, n - 1) if n - 1 <= NT else dve.wait_ge(s_x1, n - 1)
                V_.scalar_tensor_tensor(OM[n % 2], ps[:, 4 + n % 4, :], ry[:, t:t + 1], MB[0][:, 2, min(t, 1), a * 512:(a + 1) * 512],
                                        op0=ALU.mult, op1=ALU.mult).then_inc(s_om, 1)
            moe(1)

        @block.gpsimd
        def _(pool):
            for s in LED["pool"]:
                pool.sem_inc(s, 1)
            def norm_shift(nn):
                for t in range(NT):
                    pool.wait_ge(s_hm, nn // 2 * NT + t + 1)
                    nc.gpsimd.tensor_tensor(H[:, t, :], H[:, t, :], MB[nn % 2][:, 0, min(t, 1), :], ALU.add)\
                        .then_inc(s_h, 1)

            def store_modulation(q0, q1, n):
                pool.wait_ge(s_mrow, n)
                pool.dma_start(mod_d.rearrange("c l h f (m p) -> (l h f m) c p", p=P)[q0 * MB_ROWS:q1 * MB_ROWS],
                               MROW[0:(q1 - q0) * MB_ROWS]).then_inc(s_modst[n - 1], 16)

            def spread_modulation(l, half):
                if half == 0:
                    pool.dma_start(MB[0][:, 2], mod_d[:, l, 0, 2, :].partition_broadcast(P)).then_inc(s_mb[2 * l], 16)
                else:
                    for cc in range(2):
                        pool.dma_start(MB[1][:, :, cc, :], mod_d[cc, l, 1].partition_broadcast(P))\
                            .then_inc(s_mb[2 * l + 1], 16)

            nc.gpsimd.memset(mark[:, :], 0.0)
            nc.gpsimd.memset(zeros, 0.0).then_inc(s_zero, 1)

            pool.wait_ge(s_ht, NT)
            pool.dma_start(KDC[:, :, 0, :], cache_k[0, 0]).then_inc(s_kv, 16)
            pool.dma_start(KDC[:, :, 1, :], cache_k[0, 0]).then_inc(s_kv, 16)
            pool.dma_start(V[:, NT, :], cache_v[0, 0].rearrange("p g d -> p (g d)")).then_inc(s_kv, 16)
            store_modulation(0, 1, 1)
            pool.wait_ge(s_modst[0], 16)
            spread_modulation(0, 0)
            pool.wait_ge(s_gqk, 32)
            for t in range(NT):
                pool.wait_ge(s_qn, t + 1)
                nc.gpsimd.tensor_tensor(QN[:, 0:D].rearrange("p (h d) -> p h d", d=HD),
                                        QN[:, 0:D].rearrange("p (h d) -> p h d", d=HD),
                                        gqk[:, 0, :].unsqueeze(1).to_broadcast([P, NH, HD]), ALU.mult)
                nc.gpsimd.tensor_tensor(QN[:, D:QK].rearrange("p (h d) -> p h d", d=HD),
                                        QN[:, D:QK].rearrange("p (h d) -> p h d", d=HD),
                                        gqk[:, 1, :].unsqueeze(1).to_broadcast([P, NKV, HD]), ALU.mult).then_inc(s_qg, 1)
                if t >= 1:
                    pool.wait_ge(s_qg, t + 1)
                    sin = tab[:, T_SIN + (t - 1) * HD:T_SIN + t * HD].rearrange("p (a d) -> p a d", a=2)
                    qv = QN.rearrange("p (h a d) -> p a h d", a=2, d=HD // 2)
                    tv = T2.rearrange("p (h a d) -> p a h d", a=2, d=HD // 2)
                    if t >= 2:
                        pool.wait_ge(s_qf, t)
                    for a in range(2):
                        last = nc.gpsimd.tensor_tensor(tv[:, a], qv[:, 1 - a],
                                                       sin[:, a, :].unsqueeze(1).to_broadcast([P, NH + NKV, HD // 2]), ALU.mult)
                    last.then_inc(s_t2, 1)
            pool.wait_ge(s_qf, 1)
            pool.dma_start(new_k[0, 0].rearrange("p g d -> p (g d)"), KOUT).then_inc(s_out, 16)
            pool.dma_start(new_v[0, 0].rearrange("p g d -> p (g d)"), V[:, 0, :]).then_inc(s_out, 16)

            def query_columns(T):
                nc.gpsimd.tensor_copy(QC, QT[:, :, bass.ds(T * P, P)] if not isinstance(T, int)
                                      else QT[:, :, T * P:(T + 1) * P]).then_inc(s_qc, 1)

            pool.wait_ge(s_tqe, 16)
            query_columns(0)
            with pool.Fori(0, NT - 1) as i:
                pool.wait_ge(s_S, (i + 1) * NH)
                query_columns(i + 1)
            store_modulation(1, 4, 2)
            for t in range(NT):
                if t == 3:
                    pool.wait_ge(s_ot, NT)
                    pool.wait_ge(s_modst[1], 16)
                    spread_modulation(0, 1)
                    pool.dma_start(G, norm2_g[0].partition_broadcast(P)).then_inc(s_mb[1], 16)
                pool.wait_ge(s_opm, t + 1)
                nc.gpsimd.tensor_tensor(X[:, t, :], X[:, t, :], JUNK, ALU.add).then_inc(s_x1, 1)
            def moe(l):
                nn = 2 * l + 1
                norm_shift(nn)
                pool.wait_ge(ES["slot"], l + 1)
                if l == 0:
                    pool.wait_ge(s_clear, 16)
                for t in range(NT):
                    pool.wait_ge(s_h, nn * NT + t + 1)
                    for a in range(2):
                        pool.indirect_dma_start(xs_d, bass.IndirectOffsetOnAxis(ap=sloti[:, a, t:t + 1], axis=0),
                                                H[:, t, :], None).then_inc(ES["sc"], 16)
                done = 0 if l == 0 else pool.value_load(npi[0:1, 0:1], min_val=1, max_val=MAXT // 2)
                pairs = pool.value_load(npi[0:1, l:l + 1], min_val=1, max_val=MAXT // 2)
                for j in range(2):
                    pool.wait_ge(ES["yst"][j], (pairs + done) * 16 + 1)
                nc.gpsimd.tensor_tensor(mark[:, :], mark[:, :], mark[:, :], ALU.add).then_inc(ES["all"], 1)
                pool.wait_ge(ES["all"], l + 1)
                pool.wait_ge(ES["sc"], 2 * NT * 16 * (l + 1))
                for t in range(NT + 2):
                    if t >= 2:
                        pool.wait_ge(ES["wg"], l * NT + t - 1)
                        nc.gpsimd.tensor_tensor(X[:, t - 2, :], X[:, t - 2, :], GY[t % 2][1], ALU.add).then_inc(ES["x2"], 1)
                        if l == 1:
                            pool.wait_ge(ES["x2"], l * NT + t - 1)
                            pool.dma_start(y_prompt[0] if t == 2 else y_sample[0, (t - 3) * P:(t - 2) * P, :], X[:, t - 2, :])\
                                .then_inc(s_out, 16)
                    if t < NT:
                        if t >= 2:
                            pool.wait_ge(ES["x2"], l * NT + t - 1)
                        for a in range(2):
                            pool.indirect_dma_start(GY[t % 2][a], None, xs_d,
                                                    bass.IndirectOffsetOnAxis(ap=sloti[:, a, t:t + 1], axis=0))\
                                .then_inc(ES["gat"][t % 2], 16)

            moe(0)
            pool.wait_ge(s_opm, NT)
            spread_modulation(1, 0)
            P_ = nc.gpsimd
            for i in range(2):
                last = P_.memset(U[i], 0.0)
            last.then_inc(s_pad, 1)
            pool.wait_ge(s_pad, 1)
            pool.wait_ge(s_pre_dve, 4)
            pool.wait_ge(s_ssdin, 112)
            pool.wait_ge(s_ht, 3 * NT)
            with pool.Fori(0, SG) as g:
                heads = bass.ds(g * HG, HG)

                def x_times_dt(cc):
                    pool.wait_ge(s_yd, g * 5 + cc + 1)
                    for d in range(2):
                        x = P_.tensor_tensor(XS[:, d], XT[:, cc, :].rearrange("p (h n) -> p h n", h=HG),
                                             DTA[:, cc, d, heads].unsqueeze(2).to_broadcast([P, HG, SP]), ALU.mult)
                    x.then_inc(s_xs, 1)

                pool.wait_ge(s_txe, (g + 1) * 5)
                for i, (d, cc) in enumerate(UNITS):
                    if i >= 2:
                        pool.wait_ge(s_st, g * 8 + i - 1)
                    P_.tensor_tensor(XD[:, d], XT[:, cc, :].rearrange("p (h n) -> p h n", h=HG),
                                     DTD[:, cc, d, heads].unsqueeze(2).to_broadcast([P, HG, SP]), ALU.mult).then_inc(s_xsd, 1)
                for cc in range(NT):
                    x_times_dt(cc)
                    P_.tensor_tensor(Y[:, cc, bass.ds(g * 512, 512)].rearrange("p (h n) -> p h n", h=HG),
                                     XT[:, cc, :].rearrange("p (h n) -> p h n", h=HG),
                                     DROW[:, heads].unsqueeze(2).to_broadcast([P, HG, SP]), ALU.mult).then_inc(s_D, 1)
            pool.wait_ge(s_yq, SG * NT + 1)
            spread_modulation(1, 1)
            for n in range(2 * NT):
                a, t = n // NT, n % NT
                x = X[:, t, a * 512:(a + 1) * 512]
                pool.wait_ge(s_om, n + 1)
                P_.tensor_tensor(x, x, OM[n % 2], ALU.add).then_inc(s_xadd if a == 0 else s_x1, 1)
            pool.wait_ge(s_yt, 2 * NT)
            pool.dma_start(G, norm2_g[1].partition_broadcast(P)).then_inc(s_mb[3], 16)
            moe(1)
            pool.wait_ge(s_fso[0], SG * 16 + 1)
            pool.wait_ge(s_fso[1], SG * 16 + 1)
            pool.wait_ge(s_out, 16 * (NT + 2))


_INS = ["x_prompt", "x_sample", "c", "c_ctx", "cache_k", "cache_v", "state_ssm", "mod_w", "mod_b", "norm1_g",
        "norm2_g", "attn_w_qkv", "attn_q_norm_g", "attn_k_norm_g", "attn_w_o", "ssd_in_proj", "ssd_conv_w",
        "ssd_conv_b", "ssd_dt_bias", "ssd_a_log", "ssd_d", "ssd_norm_g", "ssd_out_proj", "router_w", "router_b",
        "expert_w_gate", "expert_w_up", "expert_w_down"]
_OUTS = [(1, SEQ, D), (1, DEC, D), (1, 1, SEQ, NKV, HD), (1, 1, SEQ, NKV, HD), (1, 1, 2, SH, SP, SN)]


def kernel(**inputs):
    import concourse.bacc as bacc
    from concourse.bass_utils import run_bass_kernel_spmd as run

    nc = bacc.Bacc("TRN2", target_bir_lowering=False, num_devices=1)
    arrays, args = {}, []
    for name, a in [(n, inputs[n]) for n in _INS] + [("tables", tables())]:
        a = np.ascontiguousarray(a)
        arrays[f"in_{name}"] = a
        args.append(nc.dram_tensor(f"in_{name}", a.shape, mybir.dt.from_np(a.dtype), kind="ExternalInput").ap())
    for i, shape in enumerate(_OUTS):
        args.append(nc.dram_tensor(f"out_{i}", shape, F32, kind="ExternalOutput").ap())
    backbone(nc, *args)
    r = run(nc, [arrays], core_ids=[0])
    return tuple(r.results[0][f"out_{i}"] for i in range(len(_OUTS)))
```
